# Optimizing a Trainium2 kernel written in Bass

```python
import math
import jax, jax.numpy as jnp
from jax import lax
import numpy as np

D_MODEL = 1024
BATCH = 1
SEQ = 256
DEPTH = 2

HEAD_DIM = 64
A_HEADS = 4
A_WIDTH = A_HEADS * HEAD_DIM
B_WIDTH = 256
SHORT_CONV = 3
C_WIDTH = 256
CONF_CONV = 31
D_Q_HEADS = 8
D_KV_HEADS = 2
D_GROUP = D_Q_HEADS // D_KV_HEADS
D_WIDTH = D_Q_HEADS * HEAD_DIM
D_KV_WIDTH = D_KV_HEADS * HEAD_DIM
WINDOW = 128
Q_BLOCK = 128
N_BRANCH = 4
REL_BUCKETS = 32
REL_MAX_DIST = 128
PLE_DIM = 256
D_FF = 2816
EPS = 1e-6
NEG_INF = -1e30

A_QKV_END = 3 * A_WIDTH
A_F_END = A_QKV_END + A_HEADS
B_END = A_F_END + 3 * B_WIDTH
C_END = B_END + 2 * C_WIDTH
D_END = C_END + D_WIDTH + 2 * D_KV_WIDTH
N_IN = D_END + N_BRANCH * D_MODEL

kernel_name = 'hybrid_gated_parallel_mixer'

def rms_norm(x, g):
    xf = x.astype(jnp.float32)
    y = xf * lax.rsqrt(jnp.mean(xf * xf, axis=-1, keepdims=True) + EPS)
    return (y * g.astype(jnp.float32)).astype(x.dtype)

def layer_norm(x, g, b):
    xf = x.astype(jnp.float32)
    mu = jnp.mean(xf, axis=-1, keepdims=True)
    xc = xf - mu
    y = xc * lax.rsqrt(jnp.mean(xc * xc, axis=-1, keepdims=True) + EPS)
    return (y * g.astype(jnp.float32) + b.astype(jnp.float32)).astype(x.dtype)

def swiglu_ffn(x, w_gu, w_down):
    gate, up = jnp.split(x @ w_gu, 2, axis=-1)
    return (jax.nn.silu(gate) * up) @ w_down

def causal_depthwise_conv(x, w):
    K, C = w.shape
    return lax.conv_general_dilated(
        x, w[:, None, :].astype(x.dtype), window_strides=(1,), padding=[(K - 1, 0)],
        dimension_numbers=('NWC', 'WIO', 'NWC'), feature_group_count=C)

def t5_causal_bucket(dist):
    max_exact = REL_BUCKETS // 2
    large = max_exact + (jnp.log(jnp.maximum(dist, 1).astype(jnp.float32) / max_exact)
                         / math.log(REL_MAX_DIST / max_exact)
                         * (REL_BUCKETS - max_exact)).astype(jnp.int32)
    large = jnp.minimum(large, REL_BUCKETS - 1)
    return jnp.where(dist < max_exact, dist, large)

def forgetting_attention(q, k, v, log_f):
    S, d = q.shape[1], q.shape[3]
    c = jnp.transpose(jnp.cumsum(log_f, axis=1), (0, 2, 1))
    scale = d ** -0.5
    outs = []
    for blk in range(S // Q_BLOCK):
        q0 = blk * Q_BLOCK
        end = q0 + Q_BLOCK
        s = jnp.einsum('bqhd,bkhd->bhqk', q[:, q0:end], k[:, :end]).astype(jnp.float32) * scale
        decay = c[:, :, q0:end, None] - c[:, :, None, :end]
        causal = (q0 + jnp.arange(Q_BLOCK))[:, None] >= jnp.arange(end)[None, :]
        s = jnp.where(causal, s + decay, NEG_INF)
        pr = jax.nn.softmax(s, axis=-1).astype(v.dtype)
        outs.append(jnp.einsum('bhqk,bkhd->bqhd', pr, v[:, :end]))
    return jnp.concatenate(outs, axis=1)

def sliding_window_attention(q, k, v, sinks, band_bias):
    Bn, S, _, d = q.shape
    nb = S // Q_BLOCK
    qb = q.reshape(Bn, nb, Q_BLOCK, D_KV_HEADS, D_GROUP, d)

    def band(t):
        tb = t.reshape(Bn, nb, Q_BLOCK, D_KV_HEADS, d)
        prev = jnp.concatenate([jnp.zeros_like(tb[:, :1]), tb[:, :-1]], axis=1)
        return jnp.concatenate([prev, tb], axis=2)

    kb, vb = band(k), band(v)
    s = jnp.einsum('bnqkgd,bnskd->bnkgqs', qb, kb).astype(jnp.float32) * d ** -0.5
    s = s + band_bias.reshape(D_KV_HEADS, D_GROUP, Q_BLOCK, 2 * Q_BLOCK)
    kj = jnp.arange(2 * Q_BLOCK)[None, :]
    dist = jnp.arange(Q_BLOCK)[:, None] + Q_BLOCK - kj
    in_window = (dist >= 0) & (dist < WINDOW)
    key_pos = jnp.arange(nb)[:, None] * Q_BLOCK - Q_BLOCK + kj
    valid = in_window[None] & (key_pos >= 0)[:, None, :]
    s = jnp.where(valid[None, :, None, None], s, NEG_INF)
    sink = sinks.astype(jnp.float32).reshape(1, 1, D_KV_HEADS, D_GROUP, 1, 1)
    m = jnp.maximum(jnp.max(s, axis=-1, keepdims=True), sink)
    e = jnp.exp(s - m)
    pr = (e / (jnp.sum(e, axis=-1, keepdims=True) + jnp.exp(sink - m))).astype(v.dtype)
    out = jnp.einsum('bnkgqs,bnskd->bnqkgd', pr, vb)
    return out.reshape(Bn, S, D_Q_HEADS * d)

def setup_inputs(seed: int = 0) -> dict:
    key = jax.random.key(seed)
    ks = iter(jax.random.split(key, 48))

    def nrm(shape, scale):
        return scale * jax.random.normal(next(ks), shape, jnp.float32)

    def gain(shape):
        return 1.0 + nrm(shape, 0.05)

    D, F = D_MODEL, D_FF
    return {
        'x': nrm((BATCH, SEQ, D), 1.0),
        'p': nrm((DEPTH, BATCH, SEQ, PLE_DIM), 1.0),
        'ffn1_norm_pre': gain((DEPTH, D)),
        'ffn1_w_gu': nrm((DEPTH, D, 2 * F), D ** -0.5),
        'ffn1_w_down': nrm((DEPTH, F, D), F ** -0.5),
        'ffn1_norm_post': gain((DEPTH, D)),
        'mix_norm_pre': gain((DEPTH, D)),
        'w_in': nrm((DEPTH, D, N_IN), D ** -0.5),
        'b_forget': 3.0 + nrm((DEPTH, A_HEADS), 1.0),
        'b_gate': nrm((DEPTH, N_BRANCH * D), 0.1),
        'conv_short': nrm((DEPTH, SHORT_CONV, B_WIDTH), SHORT_CONV ** -0.5),
        'conv_dw': nrm((DEPTH, CONF_CONV, C_WIDTH), CONF_CONV ** -0.5),
        'conv_dw_bias': nrm((DEPTH, C_WIDTH), 0.02),
        'conv_ln_gain': gain((DEPTH, C_WIDTH)),
        'conv_ln_bias': nrm((DEPTH, C_WIDTH), 0.02),
        'attn_sinks': nrm((DEPTH, D_Q_HEADS), 0.5),
        'rel_bias': nrm((REL_BUCKETS, D_Q_HEADS), 0.5),
        'w_br_a': nrm((DEPTH, A_WIDTH, D), A_WIDTH ** -0.5),
        'w_br_b': nrm((DEPTH, B_WIDTH, D), B_WIDTH ** -0.5),
        'w_br_c': nrm((DEPTH, C_WIDTH, D), C_WIDTH ** -0.5),
        'w_br_d': nrm((DEPTH, D_WIDTH, D), D_WIDTH ** -0.5),
        'w_o': nrm((DEPTH, D, D), D ** -0.5),
        'mix_norm_post': gain((DEPTH, D)),
        'ffn2_norm_pre': gain((DEPTH, D)),
        'ffn2_w_gu': nrm((DEPTH, D, 2 * F), D ** -0.5),
        'ffn2_w_down': nrm((DEPTH, F, D), F ** -0.5),
        'ffn2_norm_post': gain((DEPTH, D)),
        'ple_norm_gate': gain((DEPTH, D)),
        'w_ple_gate': nrm((DEPTH, D, D), D ** -0.5),
        'w_ple': nrm((DEPTH, PLE_DIM, D), PLE_DIM ** -0.5),
        'ple_norm_post': gain((DEPTH, D)),
    }

def reference(x, p, ffn1_norm_pre, ffn1_w_gu, ffn1_w_down, ffn1_norm_post,
              mix_norm_pre, w_in, b_forget, b_gate, conv_short, conv_dw, conv_dw_bias,
              conv_ln_gain, conv_ln_bias, attn_sinks, rel_bias,
              w_br_a, w_br_b, w_br_c, w_br_d, w_o, mix_norm_post,
              ffn2_norm_pre, ffn2_w_gu, ffn2_w_down, ffn2_norm_post,
              ple_norm_gate, w_ple_gate, w_ple, ple_norm_post):
    Bn, S, _ = x.shape
    band_dist = jnp.maximum(jnp.arange(Q_BLOCK)[:, None] + Q_BLOCK - jnp.arange(2 * Q_BLOCK)[None, :], 0)
    band_bias = jnp.transpose(rel_bias[t5_causal_bucket(band_dist)], (2, 0, 1)).astype(jnp.float32)

    h = x
    for i in range(DEPTH):
        f1 = swiglu_ffn(rms_norm(h, ffn1_norm_pre[i]), ffn1_w_gu[i], ffn1_w_down[i])
        h = h + 0.5 * rms_norm(f1, ffn1_norm_post[i])

        u = rms_norm(h, mix_norm_pre[i])
        proj = u @ w_in[i]
        a_qkv = proj[..., :A_QKV_END]
        a_f = proj[..., A_QKV_END:A_F_END]
        b_in = proj[..., A_F_END:B_END]
        c_in = proj[..., B_END:C_END]
        d_qkv = proj[..., C_END:D_END]
        gates = proj[..., D_END:]

        qa, ka, va = [t.reshape(Bn, S, A_HEADS, HEAD_DIM) for t in jnp.split(a_qkv, 3, axis=-1)]
        log_f = jax.nn.log_sigmoid(a_f.astype(jnp.float32) + b_forget[i].astype(jnp.float32))
        ya = forgetting_attention(qa, ka, va, log_f).reshape(Bn, S, A_WIDTH)

        bg, cg, xb = jnp.split(b_in, 3, axis=-1)
        yb = bg * causal_depthwise_conv(cg * xb, conv_short[i])

        glu = c_in[..., :C_WIDTH] * jax.nn.sigmoid(c_in[..., C_WIDTH:])
        yc = causal_depthwise_conv(glu, conv_dw[i]) + conv_dw_bias[i]
        yc = jax.nn.silu(layer_norm(yc, conv_ln_gain[i], conv_ln_bias[i]))

        qd = d_qkv[..., :D_WIDTH].reshape(Bn, S, D_Q_HEADS, HEAD_DIM)
        kd = d_qkv[..., D_WIDTH:D_WIDTH + D_KV_WIDTH].reshape(Bn, S, D_KV_HEADS, HEAD_DIM)
        vd = d_qkv[..., D_WIDTH + D_KV_WIDTH:].reshape(Bn, S, D_KV_HEADS, HEAD_DIM)
        yd = sliding_window_attention(qd, kd, vd, attn_sinks[i], band_bias)

        g = jax.nn.sigmoid(gates + b_gate[i]).reshape(Bn, S, N_BRANCH, D_MODEL)
        merged = (g[..., 0, :] * (ya @ w_br_a[i]) + g[..., 1, :] * (yb @ w_br_b[i])
                  + g[..., 2, :] * (yc @ w_br_c[i]) + g[..., 3, :] * (yd @ w_br_d[i]))
        h = h + rms_norm(merged @ w_o[i], mix_norm_post[i])

        f2 = swiglu_ffn(rms_norm(h, ffn2_norm_pre[i]), ffn2_w_gu[i], ffn2_w_down[i])
        h = h + 0.5 * rms_norm(f2, ffn2_norm_post[i])

        pg = jax.nn.sigmoid(rms_norm(h, ple_norm_gate[i]) @ w_ple_gate[i])
        h = h + pg * rms_norm(p[i] @ w_ple[i], ple_norm_post[i])
    return h


_drawn_inputs = setup_inputs


def setup_inputs(seed=0):
    import zlib

    import numpy as np

    out = dict(_drawn_inputs(seed))
    spreads = {}
    factors = {'conv_dw_bias': 2.863, 'conv_ln_bias': 6.015, 'attn_sinks': 8.0, 'ple_norm_gate': 6.13}
    for name, (base, spread) in spreads.items():
        noise = np.random.default_rng([zlib.crc32(name.encode()), seed]).standard_normal(out[name].shape)
        drawn = base * np.exp(spread * noise) if base else spread * noise
        out[name] = __import__('jax').numpy.asarray(drawn.astype(out[name].dtype))
    for name, factor in factors.items():
        out[name] = (out[name] * factor).astype(out[name].dtype)
    return out
```

```python
import math
from contextlib import ExitStack

import numpy as np

import concourse.bass as bass
from concourse import mybir

F32 = mybir.dt.float32
F32R = mybir.dt.float32r
ALU = mybir.AluOpType
ACT = mybir.ActivationFunctionType
AX = mybir.AxisListType

D = 1024
SEQ = 256
DEPTH = 2
DFF = 2816
TOK = SEQ // 128
KT = D // 128
HD = 64
AH, DH, DG = 4, 8, 4
CW = 256
KC, KS = 31, 3
EPS = 1e-6
NEG = -1e30
BUCKETS, MAXDIST, WINDOW = 32, 128, 128
QSCALE = HD ** -0.5

C_QA, C_KA, C_VA, C_F = 0, 256, 512, 768
C_BG, C_CG, C_XB = 772, 1028, 1284
C_CA, C_CB = 1540, 1796
C_QD, C_KD, C_VD = 2052, 2564, 2692
HEAD_COLS = 2820
HEAD_CHUNKS = 6
N_IN = HEAD_COLS + 4 * D

UNIT = 2048
NCH = DFF // 256
FFN_UNITS = 3 * NCH
U_FFN1 = 0
U_HEAD = U_FFN1 + FFN_UNITS
U_GATE1 = U_HEAD + 2 * HEAD_CHUNKS
U_BR_B = U_GATE1 + 8
U_BR_A = U_BR_B + 1
U_GATE2 = U_BR_A + 1
U_BR_D = U_GATE2 + 8
U_BR_C = U_BR_D + 2
U_WO = U_BR_C + 1
U_FFN2 = U_WO + 4
U_PLE = U_FFN2 + FFN_UNITS
U_PGATE = U_PLE + 1
UNITS = U_PGATE + 4
RING = 3
assert UNITS % RING == 0
UNIT_INCS = 32
GATE_ORDER = [1, 0, 3, 2]


def bucket(dist):
    exact = BUCKETS // 2
    if dist < exact:
        return dist
    return min(exact + int(math.log(dist / exact) / math.log(MAXDIST / exact) * (BUCKETS - exact)), BUCKETS - 1)


PIECES = ["A0", "A1", "D0", "D1a", "D1b"]
ROUNDS = {"A0": 1, "A1": 2, "D0": 2, "D1a": 2, "D1b": 2}
NORMS = [3, 0, 4, 8, 1, 5, 2, 6, 7]


def gate_chunk(u):
    for first, g in ((U_GATE1, 0), (U_GATE2, 4)):
        if first <= u < first + 8 and (u - first) % 2:
            return g + (u - first) // 2
    return None


def event_families():
    turns = [f"{e}_{t}{half}" for e in range(5) for t in range(TOK) for half in range(2)]
    norms = [f"{n}_{t}" for n in NORMS for t in range(TOK)]
    quarters = [f"{i}_{q}" for i in range(4) for q in range(4)]
    rounds = [f"{p}_{r}" for p in PIECES for r in range(ROUNDS[p])]
    fam = {
        "xt": turns, "xhi": turns, "xlo": turns,
        "ms": norms, "ve": norms, "rs": norms,
        "br": [x for x in quarters if x[-1] != "3"], "gb": quarters,
        "add": [f"{i}_{q}" for i in (1, 2) for q in range(4)],
        "merged_": [str(q) for q in range(4)],
        "proj": [f"{c}_{t}" for c in range(HEAD_CHUNKS) for t in range(TOK)],
        "head": [str(c) for c in range(HEAD_CHUNKS)],
        "gate": [str(g) for g in range(8)],
        "h": [f"{i}_{t}" for i in range(3) for t in range(TOK)],
        "n": [f"{i}_{t}" for i in range(3) for t in range(TOK)],
        "hg": [f"{e}_{t}" for e in (0, 1, 3, 4) for t in range(TOK)],
        "tp_": rounds, "te_": rounds,
    }
    for kind in ("sc_", "sm_", "ma_", "nm_", "ex_", "rc_", "pn_", "pv_", "yh_", "yl_"):
        fam[kind] = PIECES
    for kind in ("mb_", "sx_", "sa_"):
        fam[kind] = PIECES[2:]
    return {kind + x: (kind, n + 1, len(xs)) for kind, xs in fam.items() for n, x in enumerate(xs)}


class Events:

    def __init__(self, nc, stack):
        self.nc, self.stack, self.sems, self.places = nc, stack, {}, event_families()

    def sem(self, name):
        name = self.places[name][0] if name in self.places else name
        if name not in self.sems:
            self.sems[name] = self.stack.enter_context(self.nc.semaphore(name))
        return self.sems[name]

    def wait(self, eng, name, L, L1):
        if name in self.places:
            _, place, n = self.places[name]
            eng.wait_ge(self.sem(name), eng.snap(L * n) + place)
        else:
            eng.wait_ge(self.sem(name), L1)


def build(nc, A, out):
    stack = ExitStack()
    with stack:
        ev = Events(nc, stack)
        sem = ev.sem

        def sb(name, shape, dt=F32):
            return stack.enter_context(nc.sbuf_tensor(name, shape, dt))

        raw = sb("raw", [128, RING, UNIT])
        whi = sb("whi", [128, RING, UNIT], F32R)
        wlo = sb("wlo", [128, RING, UNIT], F32R)
        h = sb("h", [128, TOK, D])
        hg = sb("hg", [128, TOK, D])
        xhi = sb("xhi", [128, KT, SEQ], F32R)
        xlo = sb("xlo", [128, KT, SEQ], F32R)
        yhi = sb("yhi", [128, 8, SEQ], F32R)
        ylo = sb("ylo", [128, 8, SEQ], F32R)
        proj = sb("proj", [128, TOK, HEAD_COLS])
        gates = sb("gates", [128, TOK, 2 * D])
        gbias = sb("gbias", [128, 2, 512])
        gpre = sb("gpre", [128, D])
        gpost = sb("gpost", [128, D])
        qz = sb("qz", [128, DH, SEQ])
        kz = sb("kz", [128, 2, SEQ])
        S = sb("S", [128, 2, 1024])
        PT = sb("PT", [128, 8, 128])
        cumU = sb("cumU", [128, SEQ])
        maskA = sb("maskA", [128, SEQ])
        bandD = sb("bandD", [128, DH, SEQ])
        ident = sb("ident", [128, 128])
        lf = sb("lf", [128, TOK, 2, 128])
        cstc = sb("cstc", [128, 8])
        cwT = sb("cwT", [128, 2, 35])
        lnp = sb("lnp", [128, 2, CW])
        bfs = sb("bfs", [128, AH])
        snk = sb("snk", [128, DH])
        st = sb("st", [128, 160])
        epsc = sb("epsc", [128, 8])
        relT = sb("relT", [DH, BUCKETS])

        acc = proj[:, :, C_QA:C_QA + SEQ]
        bgT = proj[:, :, C_KA:C_KA + SEQ]
        upad = proj[:, :, C_BG:C_BG + SEQ + KS - 1]
        gpad = proj[:, :, C_QD:C_QD + SEQ + KC - 1]
        decL = hg[:, 1, :].rearrange("p (h q) -> p h q", h=AH)
        decR = PT[:, 2:4, :].rearrange("p a b -> p (a b)")
        cwrow = PT[0:35, 0:2, :].rearrange("p a b -> p (a b)")
        pin = gates[:, :, D:D + CW]
        silu = S[:, 0, 0:512].rearrange("p (t n) -> p t n", t=TOK)
        hact = S[:, 1, 0:512].rearrange("p (t n) -> p t n", t=TOK)
        kdup = hg[:, 0, 0:512].rearrange("p (t g r d) -> p t g r d", t=TOK, g=2, r=2)
        relrow = S[0:DH, 0, 0:512]
        relscr = nc.dram_tensor("rel_scratch", (DH, 128, 512), F32, kind="Internal").ap()

        ps = stack.enter_context(nc.psum_tensor("ps", [128, 8, 512], F32))

        def ms(s, t): return st[:, 2 * s + t:2 * s + t + 1]
        def rs(s, t): return st[:, 32 + 2 * s + t:33 + 2 * s + t]
        def ve(s, t): return st[:, 144 + t:145 + t]
        N_PRE = {0: 3, 1: 4, 3: 5, 4: 6}
        N_PLE = 7
        N_LN = 8
        def mx(p): i = PIECES.index(p); return st[:, 64 + 16 * i:64 + 16 * i + 8]
        def sums(p): i = PIECES.index(p); return st[:, 72 + 16 * i:72 + 16 * i + 8]
        sexp = sb("sexp", [128, 2, 8])

        PIECE = {
            "A0": dict(heads=[0, 1, 2, 3], qb=0, nk=1, bank=4, buf=0, pt=[7], pv=4),
            "A1": dict(heads=[0, 1, 2, 3], qb=1, nk=2, bank=5, buf=1, pt=[7, 5], pv=6),
            "D0": dict(heads=list(range(8)), qb=0, nk=1, bank=6, buf=0, pt=[4, 5], pv=6),
            "D1a": dict(heads=[0, 1, 2, 3], qb=1, nk=2, bank=4, buf=1, pt=[4, 5], pv=4),
            "D1b": dict(heads=[4, 5, 6, 7], qb=1, nk=2, bank=6, buf=0, pt=[6, 7], pv=5),
        }

        def s_view(p):
            c = PIECE[p]
            n = len(c["heads"])
            return S[:, c["buf"], 0:n * c["nk"] * 128].rearrange("p (h k) -> p h k", h=n)

        def ps_view(p):
            c = PIECE[p]
            n = len(c["heads"])
            w = n * c["nk"] * 128
            flat = ps[:, c["bank"]:c["bank"] + (w + 511) // 512, :].rearrange("p a b -> p (a b)")
            return flat[:, 0:w].rearrange("p (h k) -> p h k", h=n)

        zt = sb("zt", [128, 2, TOK, AH])
        PB = [0, 4]
        GB = [6, 2]

        def lnx(t): return proj[:, t, C_CA:C_CA + CW]
        def lnj(t): return proj[:, t, C_CB:C_CB + CW]
        lnx2 = proj[:, :, C_CA:C_CA + CW]
        lnj2 = proj[:, :, C_CB:C_CB + CW]

        def yslice(p):
            if p[0] == "A":
                return Y[0], 2, 128 * PIECE[p]["qb"]
            return Y[3] + (2 if p == "D1b" else 0), (4 if p == "D0" else 2), 128 * PIECE[p]["qb"]

        def two(bank, k=2):
            return ps[:, bank, :].rearrange("p (k n) -> p k n", k=k)

        def wide(bank):
            return ps[:, bank:bank + 2, :].rearrange("p a b -> p (a b)")

        Y = {1: 0, 0: 2, 2: 0, 3: 4}
        MERGE_W = {0: "w_br_a", 1: "w_br_b", 2: "w_br_c", 3: "w_br_d"}

        TB = {0: [[2, 3], [2, 3]], 1: [[2, 3], [2, 3]], 2: [[0, 1], [2, 3]], 3: [[4, 5], [4, 5]], 4: [[2, 3], [2, 3]]}
        FB = {0: 4, 1: 4, 2: 4}
        FB[1] = 0

        def gate_bias(eng, L, g):
            c0 = GATE_ORDER[g // 2] * D + (g % 2) * 512
            for c in (256, 0):
                src = A["b_gate"][bass.ds(L, 1), c0 + c:c0 + c + 256]
                eng.dma_start(gbias[:, g % 2, c:c + 256], src.to_broadcast([128, 256]))\
                   .then_inc(sem(f"gbias{g % 2}"), 16)

        block = stack.enter_context(nc.Block())

        @block.sync
        def _(sp):
            def bc(dst, src, name):
                return sp.dma_start(dst, src.to_broadcast([128, dst.shape[-1]])).then_inc(sem(name), 16)

            for t in range(TOK):
                sp.dma_start(h[:, t, :], A["x"][0, t * 128:(t + 1) * 128, :]).then_inc(sem("x_in"), 16)
            with nc.allow_non_contiguous_dma(reason="32 x 8 table, once"):
                sp.dma_start(relT[:, :], A["rel_bias"].rearrange("b h -> h b")).then_inc(sem("rel_in"), 16)

            with sp.Fori(0, DEPTH) as L:
                L1 = sp.snap(L + 1)
                U0 = sp.snap(L * UNITS)

                def free(u, base=None):
                    sp.wait_ge(sem("lo_ready"), (U0 if base is None else base) + (u + 1))

                def load(u, d0, s0, d1, s1, base=None):
                    free(u, base)
                    sp.dma_start(d0, s0).then_inc(sem(f"raw{u % RING}"), 16)
                    sp.dma_start(d1, s1).then_inc(sem(f"raw{u % RING}"), 16)

                def slot(u, k):
                    return raw[:, u % RING, :].rearrange("p (k n) -> p k n", k=k)

                def cols(u, w, r0, c0, n=512):
                    v = slot(u, 4)
                    load(u, v[:, 0:2, 0:n], w[L, r0:r0 + 256, c0:c0 + n].rearrange("(k p) n -> p k n", p=128),
                         v[:, 2:4, 0:n], w[L, r0 + 256:r0 + 512, c0:c0 + n].rearrange("(k p) n -> p k n", p=128))

                def rows(u, w, r0):
                    v = slot(u, 2)
                    load(u, v[:, 0, :], w[L, r0:r0 + 128, :], v[:, 1, :], w[L, r0 + 128:r0 + 256, :])

                def gate_up(u, w, half, c0, base=None):
                    v = slot(u, 4)
                    r0 = half * 512
                    load(u, v[:, :, 0:256],
                         w[L, r0:r0 + 512, bass.ds(c0, 256)].rearrange("(k p) n -> p k n", p=128),
                         v[:, :, 256:512],
                         w[L, r0:r0 + 512, bass.ds(c0 + DFF, 256)].rearrange("(k p) n -> p k n", p=128), base)

                def down(u, w, r0, base=None):
                    v = slot(u, 2)
                    load(u, v[:, 0, :], w[L, bass.ds(r0, 128), :], v[:, 1, :], w[L, bass.ds(r0 + 128, 128), :], base)

                def ffn(b, f, extra):
                    wg, wd = A[f"ffn{f}_w_gu"], A[f"ffn{f}_w_down"]
                    gate_up(b, wg, 0, 0)
                    extra(0)
                    gate_up(b + 1, wg, 1, 0)
                    gate_up(b + 2, wg, 0, 256)
                    gate_up(b + 3, wg, 1, 256)
                    extra(1)
                    down(b + 4, wd, 0)
                    with sp.Fori(2, NCH) as j:
                        Uj = sp.snap(U0 + j * 3)
                        c0 = sp.snap(j * 256)
                        r0 = sp.snap(j * 256 - 256)
                        gate_up(b - 1, wg, 0, c0, Uj)
                        gate_up(b, wg, 1, c0, Uj)
                        down(b + 1, wd, r0, Uj)
                    down(b + FFN_UNITS - 1, wd, DFF - 256)

                def small(dst, src):
                    sp.dma_start(dst, src).then_inc(sem("small"), 16)

                def extra1(i):
                    if i == 0:
                        bc(gpre[:, :], A["ffn1_norm_pre"][bass.ds(L, 1), :], "gpre0")
                        return
                    bc(gpost[:, :], A["ffn1_norm_post"][bass.ds(L, 1), :], "gpost0")
                    small(cwrow[0:KC, :], A["conv_dw"][L, :, :])
                    small(cwrow[KC:KC + KS, :], A["conv_short"][L, :, :])
                    small(cwrow[34:35, :], A["conv_dw_bias"][bass.ds(L, 1), :])
                    small(lnp[:, 0, :], A["conv_ln_gain"][bass.ds(L, 1), :].to_broadcast([128, CW]))
                    small(lnp[:, 1, :], A["conv_ln_bias"][bass.ds(L, 1), :].to_broadcast([128, CW]))
                    small(bfs[:, :], A["b_forget"][bass.ds(L, 1), :].to_broadcast([128, AH]))
                    small(snk[:, :], A["attn_sinks"][bass.ds(L, 1), :].to_broadcast([128, DH]))
                    ev.wait(sp, "hg0_1", L, L1)
                    bc(gpre[:, :], A["mix_norm_pre"][bass.ds(L, 1), :], "gpre1")

                ffn(U_FFN1, 1, extra1)

                for c in range(HEAD_CHUNKS):
                    n = min(512, HEAD_COLS - 512 * c)
                    cols(U_HEAD + 2 * c, A["w_in"], 0, 512 * c, n)
                    cols(U_HEAD + 2 * c + 1, A["w_in"], 512, 512 * c, n)
                    if c == 2:
                        ev.wait(sp, "hg1_1", L, L1)
                        bc(gpost[:, :], A["mix_norm_post"][bass.ds(L, 1), :], "gpost1")
                        bc(gpre[:, :], A["ffn2_norm_pre"][bass.ds(L, 1), :], "gpre3")
                        gate_bias(sp, L, 0)
                        gate_bias(sp, L, 1)
                for g in range(8):
                    u = (U_GATE1 if g < 4 else U_GATE2 - 8) + 2 * g
                    c0 = HEAD_COLS + GATE_ORDER[g // 2] * D + (g % 2) * 512
                    cols(u, A["w_in"], 0, c0)
                    cols(u + 1, A["w_in"], 512, c0)
                    if g == 3:
                        rows(U_BR_B, A["w_br_b"], 0)
                        rows(U_BR_A, A["w_br_a"], 0)
                rows(U_BR_D, A["w_br_d"], 0)
                rows(U_BR_D + 1, A["w_br_d"], 256)
                rows(U_BR_C, A["w_br_c"], 0)
                for i in range(4):
                    rows(U_WO + i, A["w_o"], 256 * i)

                def extra2(i):
                    if i == 1:
                        ev.wait(sp, "hg3_1", L, L1)
                        sp.dma_start(pin, A["p"][L, 0, :, :].rearrange("(t p) n -> p t n", p=128))\
                          .then_inc(sem("p_in"), 16)
                        bc(gpost[:, :], A["ffn2_norm_post"][bass.ds(L, 1), :], "gpost2")
                        bc(gpre[:, :], A["ple_norm_gate"][bass.ds(L, 1), :], "gpre4")

                ffn(U_FFN2, 2, extra2)
                rows(U_PLE, A["w_ple"], 0)
                for i in range(4):
                    rows(U_PGATE + i, A["w_ple_gate"], 256 * i)
                ev.wait(sp, "hg4_1", L, L1)
                bc(gpost[:, :], A["ple_norm_post"][bass.ds(L, 1), :], "gpost3")

            for t in range(TOK):
                sp.wait_ge(sem(f"h3_{t}"), DEPTH + 1)
                sp.dma_start(out[0, t * 128:(t + 1) * 128, :], h[:, t, :]).then_inc(sem("out"), 16)
            sp.wait_ge(sem("out"), 16 * TOK)

        @block.scalar
        def _(act):
            act.wait_ge(sem("relrow"), 1)
            act.dma_start(relscr[:, :, :], relrow.unsqueeze(1).to_broadcast([DH, 128, 512])).then_inc(sem("relscr"), 16)
            act.wait_ge(sem("relscr"), 16)
            for hh in range(DH):
                act.dma_start(bandD[:, hh, :], bass.AP(relscr.tensor, hh * 128 * 512 + 127, [[511, 128], [1, SEQ]]))\
                   .then_inc(sem("band"), 16)

            with act.Fori(0, DEPTH) as L:
                L1 = act.snap(L + 1)
                U0 = act.snap(L * UNITS)
                R0 = act.snap(L * (UNITS // RING * UNIT_INCS))
                H0 = act.snap(L * NCH)

                def after(name):
                    ev.wait(act, name, L, L1)

                def used(u):
                    act.wait_ge(sem("unit_used"), U0 + (u + 1 + RING))

                def hi(u, n=512):
                    act.wait_ge(sem(f"raw{u % RING}"), R0 + UNIT_INCS * (u // RING + 1))
                    act.wait_ge(sem("unit_used"), U0 + (u + 1))
                    s, d = (v[:, u % RING, :].rearrange("p (k n) -> p k n", k=4)[:, :, 0:n] for v in (raw, whi))
                    act.activation(d, s, ACT.Copy).then_inc(sem("hi_ready"), 1)

                def hi_j(u, Uj, Rj):
                    act.wait_ge(sem(f"raw{u % RING}"), Rj + UNIT_INCS * (u // RING + 1))
                    act.wait_ge(sem("unit_used"), Uj + (u + 1))
                    act.activation(whi[:, u % RING, :], raw[:, u % RING, :], ACT.Copy).then_inc(sem("hi_ready"), 1)

                def mean_square(dst, src, width, junk, name):
                    act.activation(junk, src, ACT.Square, scale=width ** -0.5, accum_out=dst)\
                       .then_inc(sem(name), 1)

                def copy(dst, src, wait, name, scale=1.0):
                    after(wait)
                    act.activation(dst, src, ACT.Copy, scale=scale).then_inc(sem(name), 1)

                def transposed(e, t):
                    for half in range(2):
                        copy(xhi[:, 4 * half:4 * half + 4, t * 128:(t + 1) * 128], two(TB[e][t][half], 4),
                             f"xt{e}_{t}{half}", f"xhi{e}_{t}{half}")

                def pre_stats(e, hname):
                    for t in range(TOK):
                        after(f"{hname}_{t}")
                        mean_square(ms(N_PRE[e], t), h[:, t, :], D, gates[:, t, 0:D], f"ms{N_PRE[e]}_{t}")

                def boundary(s, e, last):
                    for t in range(TOK):
                        after(f"f{s}_0") if t == 0 else used(last)
                        mean_square(ms(s, t), wide(FB[s] + 2 * t), D, hg[:, t, :], f"ms{s}_{t}")
                    for t in range(TOK):
                        transposed(e, t)
                    pre_stats(e, f"h{s}")

                def ffn(b, f, e):
                    def gate(tok, j, u=None, Uj=None):
                        if tok == 0:
                            act.wait_ge(sem(f"gu{f}"), j)
                        else:
                            act.wait_ge(sem("unit_used"), (U0 if Uj is None else Uj) + (u + 1 + RING))
                        act.activation(silu[:, tok, :], ps[:, tok, 0:256], ACT.Silu,
                                       scale=rs(N_PRE[e], tok)).then_inc(sem(f"silu{f}_{tok}"), 1)

                    def hidden(j, buf):
                        act.wait_ge(sem(f"ht{f}"), j)
                        act.activation(yhi[:, 2 * buf:2 * buf + 2, :], two(2), ACT.Copy).then_inc(sem(f"hthi{f}"), 1)

                    hi(b + 2)
                    hi(b + 3)
                    for t in range(TOK):
                        after(f"rs{N_PRE[e]}_{t}")
                        gate(t, H0 + 1, b + 1)
                    hi(b + 4)
                    hidden(H0 + 1, 0)
                    hi(b + 5)
                    for t in range(TOK):
                        gate(t, H0 + 2, b + 3)
                    hi(b + 6)
                    hi(b + 7)
                    with act.Fori(2, NCH - 1) as j:
                        Hj = act.snap(H0 + j)
                        Uj = act.snap(U0 + j * 3)
                        Rj = act.snap(R0 + j * UNIT_INCS)
                        hidden(Hj, 0)
                        hi_j(b + 2, Uj, Rj)
                        for t in range(TOK):
                            gate(t, Hj + 1, b, Uj)
                        hi_j(b + 3, Uj, Rj)
                        hi_j(b + 4, Uj, Rj)
                    hidden(H0 + NCH - 1, 0)
                    hi(b + 32)
                    for t in range(TOK):
                        gate(t, H0 + NCH, b + 30)
                    hi(b + 33)
                    hidden(H0 + NCH, 1)
                    hi(b + 34)

                def exps(p):
                    c = PIECE[p]
                    v = s_view(p)
                    n = len(c["heads"])
                    after(f"nm_{p}")
                    for i in range(n):
                        ins = act.activation(v[:, i, :], v[:, i, :], ACT.Exp, bias=mx(p)[:, i:i + 1],
                                             accum_out=sums(p)[:, i:i + 1])
                    ins.then_inc(sem(f"ex_{p}"), 1)
                    if p[0] == "D":
                        act.activation(sexp[:, c["buf"], 0:n], sexp[:, c["buf"], 0:n], ACT.Exp)\
                           .then_inc(sem(f"sx_{p}"), 1)

                def probs_t(p, r):
                    n = min(4, len(PIECE[p]["heads"]) * PIECE[p]["nk"] - 4 * r)
                    copy(PT[:, 4 * r:4 * r + n, :], two(PIECE[p]["pt"][r], 4)[:, 0:n, :], f"tp_{p}_{r}", f"te_{p}_{r}")

                def y_hi(p):
                    y0, n, q = yslice(p)
                    copy(yhi[:, y0:y0 + n, q:q + 128],
                         ps[:, PIECE[p]["pv"], 0:n * 128].rearrange("p (k n) -> p k n", k=n), f"pv_{p}", f"yh_{p}")

                def queries(bank, h0, name):
                    v = two(bank)
                    act.activation(qz[0:64, h0:h0 + 4:2, :], v[0:64], ACT.Copy, scale=QSCALE)
                    act.activation(qz[64:128, h0 + 1:h0 + 4:2, :], v[64:128], ACT.Copy, scale=QSCALE)\
                       .then_inc(sem(name), 1)

                def sigmoid_gates(first_chunk, i):
                    act.wait_ge(sem("gate_pre"), act.snap(L * 16) + (2 * first_chunk + 4))
                    act.activation(gates[:, :, (i % 2) * D:(i % 2 + 1) * D], gates[:, :, (i % 2) * D:(i % 2 + 1) * D],
                                   ACT.Sigmoid).then_inc(sem(f"sig{i}"), 1)

                hi(0)
                hi(1)
                for t in range(TOK):
                    transposed(0, t)
                pre_stats(0, "h3")
                ffn(U_FFN1, 1, 0)
                boundary(0, 1, U_HEAD - 1)

                for u in range(U_HEAD, U_WO + 4):
                    if u + 2 < U_WO + 6:
                        hi(u + 2, HEAD_COLS - 5 * 512 if u + 2 in (U_GATE1 - 2, U_GATE1 - 1) else 512)
                    if U_HEAD <= u < U_GATE1 and (u - U_HEAD) % 2:
                        c = (u - U_HEAD) // 2
                        n = min(512, HEAD_COLS - 512 * c)
                        for t in range(TOK):
                            after(f"rs{N_PRE[1]}_{t}")
                            after(f"head{c}") if t == 0 else used(u)
                            act.activation(proj[:, t, 512 * c:512 * c + n], ps[:, 2 * (c % 2) + t, 0:n],
                                           ACT.Copy, scale=rs(N_PRE[1], t)).then_inc(sem(f"proj{c}_{t}"), 1)
                    g = gate_chunk(u - 2)
                    if g is not None and g < 6:
                        act.wait_ge(sem("gate_pre"), act.snap(L * 16) + (2 * g + 2))
                        gate_bias(act, L, g + 2)
                    if u == 37:
                        after("z")
                        act.activation(zt[:, 1], zt[:, 0], ACT.Abs).then_inc(sem("zabs"), 1)
                        after("zabs")
                        act.activation(zt[:, 1], zt[:, 1], ACT.Exp, scale=-1.0).then_inc(sem("zexp"), 1)
                        after("zexp")
                        act.activation(zt[:, 1], zt[:, 1], ACT.Ln, bias=1.0).then_inc(sem("zln"), 1)
                    if u == 39:
                        after("tA")
                        queries(4, 0, "qA")
                        copy(kz[:, :, :], two(5), "tA", "kA")
                    if u == 42:
                        exps("A0")
                    if u == 43:
                        exps("A1")
                    if u == 44:
                        probs_t("A0", 0)
                    if u == 45:
                        y_hi("A0")
                        probs_t("A1", 0)
                        probs_t("A1", 1)
                    if u == 46:
                        y_hi("A1")
                        for t in range(TOK):
                            after(f"proj4_{t}")
                        act.activation(lnj2, lnj2, ACT.Sigmoid).then_inc(sem("csig"), 1)
                        for t in range(TOK):
                            after(f"proj5_{t}")
                        for t in range(TOK):
                            ins = act.activation(kdup[:, t], proj[:, t, C_KD:C_KD + 128]
                                                 .rearrange("p (g d) -> p g d", g=2).unsqueeze(2)
                                                 .to_broadcast([128, 2, 2, HD]), ACT.Copy)
                        ins.then_inc(sem("kdup"), 1)
                    if u == 47:
                        copy(upad[:, :, KS - 1:], two(4), "tB", "uT")
                        copy(bgT[:, :, :], two(5), "tB", "bgT")
                    if u == 48:
                        after("tD")
                        queries(6, 0, "qD0")
                        queries(7, 4, "qD1")
                    if u == 49:
                        copy(kz[:, :, :], two(4), "tDk", "kD")
                        copy(gpad[:, :, KC - 1:], two(5), "tC", "gT")
                    if u == 50:
                        copy(yhi[:, Y[1]:Y[1] + 2, :], acc[:, :, :], "yb", "ybh")
                    if u == 51:
                        exps("D0")
                    if u == 52:
                        probs_t("D0", 0)
                        probs_t("D0", 1)
                        for i in range(2):
                            sigmoid_gates(2 * i, i)
                    if u == 53:
                        y_hi("D0")
                    if u == 57:
                        exps("D1a")
                    if u == 58:
                        exps("D1b")
                    if u == 59:
                        probs_t("D1a", 0)
                        probs_t("D1a", 1)
                    if u == 60:
                        y_hi("D1a")
                    if u == 61:
                        probs_t("D1b", 0)
                        probs_t("D1b", 1)
                    if u == 62:
                        y_hi("D1b")
                        for t in range(TOK):
                            after(f"xc{t}")
                            mean_square(ms(N_LN, t), lnx(t), CW, lnj(t), f"ms{N_LN}_{t}")
                        for i in range(2):
                            sigmoid_gates(4 + 2 * i, 2 + i)
                    if u == 63:
                        after("lny")
                        act.activation(lnj2, lnx2, ACT.Sigmoid).then_inc(sem("lnsig"), 1)
                    if u == 64:
                        copy(yhi[:, Y[2]:Y[2] + 2, :], two(7), "t6", "ych")
                    if u == 65:
                        for t in range(TOK):
                            transposed(2, t)
                boundary(1, 3, U_FFN2 - 1)

                ffn(U_FFN2, 2, 3)
                copy(yhi[:, 4:6, :], two(3), "tp", "ph")
                boundary(2, 4, U_PLE - 1)
                for u in range(U_PGATE + 1, UNITS):
                    hi(u)
                for t in range(TOK):
                    after(f"ms{N_PRE[4]}_{t}")
                    after("pd") if t == 0 else used(U_PLE)
                    mean_square(ms(N_PLE, t), wide(PB[t]), D, gates[:, t, 0:D], f"ms{N_PLE}_{t}")
                for t in range(TOK):
                    after(f"rs{N_PRE[4]}_{t}")
                    after("gd") if t == 0 else used(UNITS - 1)
                    act.activation(gates[:, t, D:2 * D], wide(GB[t]), ACT.Sigmoid,
                                   scale=rs(N_PRE[4], t)).then_inc(sem(f"pg_{t}"), 1)

        @block.vector
        def _(dve):
            dve.memset(st[:, 0:40], 0.0).then_inc(sem("lo_ready"), RING)
            dve.memset(st[:, 40:80], 0.0).then_inc(sem("unit_used"), RING)
            dve.memset(st[:, 80:160], 0.0)
            dve.memset(lf[:, :, :, :], 0.0).then_inc(sem("lf0"), 1)
            dve.memset(qz[:, :, :], 0.0).then_inc(sem("qz0"), 1)
            dve.memset(relrow, NEG).then_inc(sem("rel0"), 1)
            dve.wait_ge(sem("rel0"), 1)
            dve.wait_ge(sem("rel_in"), 16)
            lo_d = 0
            while lo_d < WINDOW:
                hi_d = lo_d
                while hi_d < WINDOW and bucket(hi_d) == bucket(lo_d):
                    hi_d += 1
                b = bucket(lo_d)
                ins = dve.tensor_copy(relrow[:, 256 - hi_d:256 - lo_d],
                                      relT[:, b:b + 1].to_broadcast([DH, hi_d - lo_d]))
                lo_d = hi_d
            ins.then_inc(sem("relrow"), 1)
            dve.wait_ge(sem("x_in"), 16 * TOK)
            for t in range(TOK):
                dve.memset(zt[:, t], 0.0).then_inc(sem(f"h3_{t}"), 1)
            dve.wait_ge(sem("relscr"), 16)
            dve.wait_ge(sem("band"), 16 * DH)
            dve.wait_ge(sem("masks"), 1)

            with dve.Fori(0, DEPTH) as L:
                L1 = dve.snap(L + 1)
                L16 = dve.snap(L * 16 + 16)
                U0 = dve.snap(L * UNITS)
                H0 = dve.snap(L * NCH)

                def after(name):
                    ev.wait(dve, name, L, L1)

                def used(u):
                    dve.wait_ge(sem("unit_used"), U0 + (u + 1 + RING))

                def lo(u, n=512, Uj=None):
                    dve.wait_ge(sem("hi_ready"), (U0 if Uj is None else Uj) + (u + 1))
                    d, a, b = (v[:, u % RING, :].rearrange("p (k n) -> p k n", k=4)[:, :, 0:n]
                               for v in (wlo, raw, whi))
                    dve.tensor_tensor(d, a, b, ALU.subtract).then_inc(sem("lo_ready"), 1)

                def minus(dst, a, b, wait, name):
                    after(wait)
                    dve.tensor_tensor(dst, a, b, ALU.subtract).then_inc(sem(name), 1)

                def transposed(e, t):
                    for half in range(2):
                        k, q = slice(4 * half, 4 * half + 4), slice(t * 128, (t + 1) * 128)
                        minus(xlo[:, k, q], two(TB[e][t][half], 4), xhi[:, k, q],
                              f"xhi{e}_{t}{half}", f"xlo{e}_{t}{half}")

                def premult(e, t, hname):
                    dve.wait_ge(sem(f"gpre{e}"), L16)
                    after(f"{hname}_{t}")
                    dve.tensor_tensor(hg[:, t, :], h[:, t, :], gpre[:, :], ALU.mult).then_inc(sem(f"hg{e}_{t}"), 1)

                def post1(s, t):
                    dve.wait_ge(sem(f"gpost{s}"), L16)
                    after(f"rs{s}_{t}")
                    dve.scalar_tensor_tensor(out=hg[:, t, :], in0=wide(FB[s] + 2 * t), scalar=rs(s, t),
                                             in1=gpost[:, :], op0=ALU.mult, op1=ALU.mult).then_inc(sem(f"n{s}_{t}"), 1)

                def post2(s, t):
                    after(f"n{s}_{t}")
                    dve.scalar_tensor_tensor(out=h[:, t, :], in0=hg[:, t, :], scalar=1.0 if s == 1 else 0.5,
                                             in1=h[:, t, :], op0=ALU.mult, op1=ALU.add).then_inc(sem(f"h{s}_{t}"), 1)

                def boundary(s, e):
                    post1(s, 0)
                    post2(s, 0)
                    premult(e, 0, f"h{s}")
                    post1(s, 1)
                    transposed(e, 0)
                    post2(s, 1)
                    premult(e, 1, f"h{s}")
                    transposed(e, 1)

                def ffn(b, f, e):
                    def act_up(tok, j):
                        dve.wait_ge(sem(f"silu{f}_{tok}"), j)
                        dve.scalar_tensor_tensor(out=hact[:, tok, :], in0=ps[:, tok, 256:512],
                                                 scalar=rs(N_PRE[e], tok), in1=silu[:, tok, :],
                                                 op0=ALU.mult, op1=ALU.mult).then_inc(sem(f"hact{f}_{tok}"), 1)

                    def hidden(j, buf):
                        dve.wait_ge(sem(f"hthi{f}"), j)
                        dve.tensor_tensor(ylo[:, 2 * buf:2 * buf + 2, :], two(2), yhi[:, 2 * buf:2 * buf + 2, :],
                                          ALU.subtract).then_inc(sem(f"htlo{f}"), 1)

                    lo(b + 2)
                    lo(b + 3)
                    for t in range(TOK):
                        act_up(t, H0 + 1)
                    lo(b + 4)
                    hidden(H0 + 1, 0)
                    lo(b + 5)
                    for t in range(TOK):
                        act_up(t, H0 + 2)
                    lo(b + 6)
                    lo(b + 7)
                    with dve.Fori(2, NCH - 1) as j:
                        Hj = dve.snap(H0 + j)
                        Uj = dve.snap(U0 + j * 3)
                        hidden(Hj, 0)
                        lo(b + 2, Uj=Uj)
                        for t in range(TOK):
                            act_up(t, Hj + 1)
                        lo(b + 3, Uj=Uj)
                        lo(b + 4, Uj=Uj)
                    hidden(H0 + NCH - 1, 0)
                    lo(b + 32)
                    for t in range(TOK):
                        act_up(t, H0 + NCH)
                    lo(b + 33)
                    hidden(H0 + NCH, 1)
                    lo(b + 34)

                def softmax_in(p):
                    c = PIECE[p]
                    n, nk, v = len(c["heads"]), c["nk"], s_view(p)
                    after(f"sc_{p}")
                    if p[0] == "A":
                        m = maskA[:, SEQ - 128 * nk:].unsqueeze(1).to_broadcast([128, n, 128 * nk])
                    else:
                        m = bandD[:, c["heads"][0]:c["heads"][0] + n, SEQ - 128 * nk:]
                    dve.tensor_tensor(v, ps_view(p), m, ALU.add).then_inc(sem(f"sm_{p}"), 1)
                    after(f"sm_{p}")
                    dve.tensor_reduce(sums(p)[:, 0:n], v, AX.X, ALU.max).then_inc(sem(f"ma_{p}"), 1)
                    after(f"ma_{p}")
                    if p[0] == "A":
                        dve.tensor_scalar(mx(p)[:, 0:n], sums(p)[:, 0:n], -1.0, None, ALU.mult)\
                           .then_inc(sem(f"nm_{p}"), 1)
                        return
                    sk = snk[:, c["heads"][0]:c["heads"][0] + n]
                    dve.tensor_tensor(sums(p)[:, 0:n], sums(p)[:, 0:n], sk, ALU.max).then_inc(sem(f"mb_{p}"), 1)
                    after(f"mb_{p}")
                    dve.tensor_tensor(sexp[:, c["buf"], 0:n], sk, sums(p)[:, 0:n], ALU.subtract)
                    dve.tensor_scalar(mx(p)[:, 0:n], sums(p)[:, 0:n], -1.0, None, ALU.mult)\
                       .then_inc(sem(f"nm_{p}"), 1)

                def softmax_out(p):
                    c = PIECE[p]
                    n = len(c["heads"])
                    if p[0] == "D":
                        after(f"sx_{p}")
                        dve.tensor_tensor(sums(p)[:, 0:n], sums(p)[:, 0:n], sexp[:, c["buf"], 0:n], ALU.add)\
                           .then_inc(sem(f"sa_{p}"), 1)
                        after(f"sa_{p}")
                    else:
                        after(f"ex_{p}")
                    dve.reciprocal(sums(p)[:, 0:n], sums(p)[:, 0:n]).then_inc(sem(f"rc_{p}"), 1)

                def y_lo(p):
                    y0, n, q = yslice(p)
                    minus(ylo[:, y0:y0 + n, q:q + 128],
                          ps[:, PIECE[p]["pv"], 0:n * 128].rearrange("p (k n) -> p k n", k=n),
                          yhi[:, y0:y0 + n, q:q + 128], f"yh_{p}", f"yl_{p}")

                def tap(k, src, row, base, name, bias):
                    for c in range(2):
                        x, w = src[:, c, k:k + SEQ], cwT[:, c, row + k:row + k + 1]
                        if k == 0:
                            if bias:
                                ins = dve.tensor_scalar(acc[:, c, :], x, w, cwT[:, c, 34:35], ALU.mult, ALU.add)
                            else:
                                ins = dve.tensor_scalar(acc[:, c, :], x, w, None, ALU.mult)
                        else:
                            dve.wait_ge(sem(f"{name}{c}"), base + k)
                            ins = dve.scalar_tensor_tensor(out=acc[:, c, :], in0=x, scalar=w, in1=acc[:, c, :],
                                                           op0=ALU.mult, op1=ALU.add)
                        ins.then_inc(sem(f"{name}{c}"), 1)

                def branch(i, u, gate_slot, bank):
                    after(f"sig{i}")
                    for q in range(4):
                        after(f"br{i}_{q}") if q < 3 else used(u)
                        t, n = q // 2, q % 2
                        g = gates[:, t, gate_slot * D + n * 512:gate_slot * D + n * 512 + 512]
                        m = hg[:, t, n * 512:n * 512 + 512]
                        dve.tensor_tensor(m if i == 0 else g, ps[:, bank + q, :], g, ALU.mult)\
                           .then_inc(sem(f"gb{i}_{q}"), 1)
                        if i == 3:
                            after(f"add2_{q}")
                            after(f"gb{i}_{q}")
                            dve.tensor_tensor(m, m, g, ALU.add).then_inc(sem(f"merged_{q}"), 1)

                premult(0, 0, "h3")
                premult(0, 1, "h3")
                lo(0)
                transposed(0, 0)
                lo(1)
                transposed(0, 1)
                ffn(U_FFN1, 1, 0)
                boundary(0, 1)

                C0 = dve.snap(L * KC)
                B0 = dve.snap(L * KS)
                dve.wait_ge(sem("small"), dve.snap(L * (16 * 7)) + 16 * 7)
                for u in range(U_HEAD, U_WO + 4):
                    lo(u + 2, HEAD_COLS - 5 * 512 if u + 2 in (U_GATE1 - 2, U_GATE1 - 1) else 512)
                    g = gate_chunk(u)
                    if g is not None:
                        dve.wait_ge(sem(f"gbias{g % 2}"), dve.snap(L * 128) + 32 * (g // 2 + 1))
                        if g == 6:
                            after("add1_3")
                        for t in range(TOK):
                            after(f"gate{g}") if t == 0 else used(u)
                            dve.scalar_tensor_tensor(
                                out=gates[:, t, (g % 4) * 512:(g % 4) * 512 + 512], in0=ps[:, 2 * (g % 2) + t, :],
                                scalar=rs(N_PRE[1], t), in1=gbias[:, g % 2, :],
                                op0=ALU.mult, op1=ALU.add).then_inc(sem("gate_pre"), 1)
                    if u == 37:
                        for t in range(TOK):
                            after(f"proj1_{t}")
                        dve.tensor_tensor(zt[:, 0], proj[:, :, C_F:C_F + AH],
                                          bfs[:, :].unsqueeze(1).to_broadcast([128, TOK, AH]), ALU.add)\
                           .then_inc(sem("z"), 1)
                    if u == 38:
                        after("zln")
                        dve.tensor_scalar(zt[:, 0], zt[:, 0], 0.0, None, ALU.min).then_inc(sem("zmin"), 1)
                        after("zmin")
                        dve.tensor_tensor(lf[:, :, 0, 0:AH], zt[:, 1], zt[:, 0], ALU.subtract)
                        dve.tensor_tensor(lf[:, :, 1, AH:2 * AH], zt[:, 0], zt[:, 1], ALU.subtract)\
                           .then_inc(sem("lf"), 1)
                    if u == 40:
                        after("cs")
                        dve.tensor_scalar(decR[:, :], ps[:, 6, 0:SEQ], cstc[:, 0:1], None, ALU.add)
                        for hh in range(AH):
                            ins = dve.tensor_scalar(decL[:, hh, :], ps[:, 6, SEQ:], cstc[:, 1:2],
                                                    cstc[:, 2 + hh:3 + hh], ALU.add, ALU.mult)
                        ins.then_inc(sem("dec"), 1)
                        after("tcw")
                        dve.tensor_copy(cwT[:, :, :], ps[:, 7, 0:70].rearrange("p (k n) -> p k n", k=2))\
                           .then_inc(sem("cw"), 1)
                    if u == 42:
                        softmax_in("A0")
                        softmax_in("A1")
                    if u == 43:
                        softmax_out("A0")
                        softmax_out("A1")
                    if u == 45:
                        y_lo("A0")
                    if u == 46:
                        y_lo("A1")
                    if u == 48:
                        after("uT")
                        after("cw")
                        dve.memset(upad[:, :, 0:KS - 1], 0.0).then_inc(sem("pad0"), 1)
                        after("pad0")
                        for k in range(KS):
                            tap(k, upad, KC, B0, "cb", False)
                        after("bgT")
                        for c in range(2):
                            dve.wait_ge(sem(f"cb{c}"), B0 + KS)
                        dve.tensor_tensor(acc[:, :, :], acc[:, :, :], bgT[:, :, :], ALU.mult).then_inc(sem("yb"), 1)
                    if u == 50:
                        minus(ylo[:, Y[1]:Y[1] + 2, :], acc[:, :, :], yhi[:, Y[1]:Y[1] + 2, :], "ybh", "ybl")
                        softmax_in("D0")
                    if u == 51:
                        softmax_out("D0")
                        after("gT")
                        dve.memset(gpad[:, :, 0:KC - 1], 0.0).then_inc(sem("pad1"), 1)
                        after("ybl")
                        after("pad1")
                    if 51 <= u < 61:
                        k0 = 3 * (u - 51)
                        for k in range(k0, KC if u == 60 else k0 + 3):
                            tap(k, gpad, 0, C0, "cc", True)
                    if u == 53:
                        y_lo("D0")
                        branch(0, U_BR_B, 0, 0)
                    if u == 54:
                        branch(1, U_BR_A, 1, 4)
                    if u == 56:
                        softmax_in("D1a")
                    if u == 57:
                        softmax_out("D1a")
                        softmax_in("D1b")
                    if u == 58:
                        softmax_out("D1b")
                    if u == 60:
                        y_lo("D1a")
                    if u == 62:
                        y_lo("D1b")
                        after("t5")
                        dve.tensor_reduce(st[:, 146:148], two(6), AX.X, ALU.add).then_inc(sem("lnsum"), 1)
                        after("lnsum")
                        dve.tensor_scalar(st[:, 148:150], st[:, 146:148], -1.0 / CW, None, ALU.mult)\
                           .then_inc(sem("lnmean"), 1)
                        after("lnmean")
                        for t in range(TOK):
                            dve.tensor_scalar(lnx(t), two(6)[:, t, :], st[:, 148 + t:149 + t], None, ALU.add)\
                               .then_inc(sem(f"xc{t}"), 1)
                        for t in range(TOK):
                            after(f"rs{N_LN}_{t}")
                            dve.scalar_tensor_tensor(out=lnx(t), in0=lnx(t), scalar=rs(N_LN, t), in1=lnp[:, 0, :],
                                                     op0=ALU.mult, op1=ALU.mult).then_inc(sem(f"lng{t}"), 1)
                    if u == 64:
                        minus(ylo[:, Y[2]:Y[2] + 2, :], two(7), yhi[:, Y[2]:Y[2] + 2, :], "ych", "ycl")
                        branch(2, U_BR_D + 1, 0, 0)
                    if u == 65:
                        branch(3, U_BR_C, 1, 4)
                        for t in range(TOK):
                            transposed(2, t)
                boundary(1, 3)

                ffn(U_FFN2, 2, 3)
                minus(ylo[:, 4:6, :], two(3), yhi[:, 4:6, :], "ph", "pl")
                boundary(2, 4)
                for u in range(U_PGATE + 1, UNITS):
                    lo(u)
                dve.wait_ge(sem("gpost3"), L16)
                for t in range(TOK):
                    after(f"rs{N_PLE}_{t}")
                    dve.scalar_tensor_tensor(out=gates[:, t, 0:D], in0=wide(PB[t]), scalar=rs(N_PLE, t),
                                             in1=gpost[:, :], op0=ALU.mult, op1=ALU.mult).then_inc(sem(f"pn_{t}"), 1)
                for t in range(TOK):
                    after(f"pn_{t}")
                    after(f"pg_{t}")
                    dve.tensor_tensor(gates[:, t, 0:D], gates[:, t, 0:D], gates[:, t, D:2 * D], ALU.mult)\
                       .then_inc(sem(f"pp_{t}"), 1)
                    after(f"pp_{t}")
                    dve.tensor_tensor(h[:, t, :], h[:, t, :], gates[:, t, 0:D], ALU.add).then_inc(sem(f"h3_{t}"), 1)

        @block.gpsimd
        def _(pool):
            pool.memset(epsc[:, 0:4], EPS).then_inc(sem("c_eps"), 1)
            pool.memset(epsc[:, 4:8], -0.5).then_inc(sem("c_half"), 1)
            pool.memset(ident[:, :], 0.0).then_inc(sem("c_id"), 1)
            pool.memset(cumU[:, :], 1.0).then_inc(sem("c_u"), 1)
            pool.memset(maskA[:, :], 0.0).then_inc(sem("c_m"), 1)
            pool.memset(cstc[:, 0:2], 1.0).then_inc(sem("c_c"), 1)
            pool.memset(cstc[:, 2:8], 0.0).then_inc(sem("c_c"), 1)
            for name, n in (("c_eps", 1), ("c_half", 1), ("c_id", 1), ("c_u", 1), ("c_m", 1), ("c_c", 2)):
                pool.wait_ge(sem(name), n)

            def select(ap, op, fill, base, pattern, cm):
                return pool.affine_select(out=ap, in_=ap, compare_op=op, fill=fill, base=base, pattern=pattern,
                                          channel_multiplier=cm)

            select(ident[:, :], ALU.not_equal, 1.0, 0, [[-1, 128]], 1).then_inc(sem("ident"), 1)
            select(cumU[:, :], ALU.is_ge, 0.0, 0, [[1, SEQ]], -1)
            select(maskA[:, :], ALU.is_ge, NEG, 128, [[-1, SEQ]], 1)
            select(cstc[:, 0:1], ALU.is_ge, 0.0, -AH, [[0, 1]], 1).then_inc(sem("c_c"), 1)
            select(cstc[:, 1:2], ALU.is_ge, 0.0, AH - 1, [[0, 1]], -1).then_inc(sem("c_c"), 1)
            select(cstc[:, 2:6], ALU.not_equal, 1.0, 0, [[-1, AH]], 1).then_inc(sem("c_c"), 1)
            pool.wait_ge(sem("c_c"), 5)
            select(cstc[:, 0:1], ALU.is_ge, 0.0, 2 * AH - 1, [[0, 1]], -1).then_inc(sem("c_c"), 1)
            pool.wait_ge(sem("c_c"), 6)
            select(cstc[:, 2:6], ALU.not_equal, 1.0, -AH, [[-1, AH]], 1).then_inc(sem("masks"), 1)

            with pool.Fori(0, DEPTH) as L:
                L1 = pool.snap(L + 1)

                def after(name):
                    ev.wait(pool, name, L, L1)

                def root(s):
                    for t in range(TOK):
                        after(f"ms{s}_{t}")
                        pool.tensor_tensor(ve(s, t), ms(s, t), epsc[:, 0:1], ALU.add).then_inc(sem(f"ve{s}_{t}"), 1)
                        after(f"ve{s}_{t}")
                        pool.tensor_tensor(rs(s, t), ve(s, t), epsc[:, 4:5], ALU.pow).then_inc(sem(f"rs{s}_{t}"), 1)

                def tt(dst, a, b, op, name):
                    pool.tensor_tensor(dst, a, b, op).then_inc(sem(name), 1)

                def normalise(p):
                    after(f"rc_{p}")
                    v = s_view(p)
                    n, w = len(PIECE[p]["heads"]), 128 * PIECE[p]["nk"]
                    tt(v, v, sums(p)[:, 0:n].unsqueeze(2).to_broadcast([128, n, w]), ALU.mult, f"pn_{p}")

                def add_branch(i, gate_slot):
                    for q in range(4):
                        after(f"gb{i}_{q}")
                        t, n = q // 2, q % 2
                        m = hg[:, t, n * 512:n * 512 + 512]
                        tt(m, m, gates[:, t, gate_slot * D + n * 512:gate_slot * D + n * 512 + 512], ALU.add,
                           f"add{i}_{q}")

                root(N_PRE[0])
                root(0)
                root(N_PRE[1])
                normalise("A0")
                normalise("A1")
                for t in range(TOK):
                    after(f"proj3_{t}")
                xb = proj[:, :, C_XB:C_XB + CW]
                tt(xb, xb, proj[:, :, C_CG:C_CG + CW], ALU.mult, "cgxb")
                after("csig")
                tt(lnx2, lnx2, lnj2, ALU.mult, "glu")
                normalise("D0")
                add_branch(1, 1)
                normalise("D1a")
                normalise("D1b")
                root(N_LN)
                for t in range(TOK):
                    after(f"lng{t}")
                tt(lnx2, lnx2, lnp[:, 1, :].unsqueeze(1).to_broadcast([128, TOK, CW]), ALU.add, "lny")
                after("lnsig")
                tt(lnx2, lnx2, lnj2, ALU.mult, "lnm")
                add_branch(2, 0)
                root(1)
                root(N_PRE[3])
                root(2)
                root(N_PRE[4])
                root(N_PLE)

        @block.tensor
        def _(pe):
            with pe.Fori(0, DEPTH) as L:
                L1 = pe.snap(L + 1)
                U0 = pe.snap(L * UNITS)
                H0 = pe.snap(L * NCH)
                G0 = pe.snap(L * 16)

                def after(name):
                    ev.wait(pe, name, L, L1)

                def split(u, Uj=None):
                    pe.wait_ge(sem("lo_ready"), (U0 if Uj is None else Uj) + (u + 1 + RING))

                def mm(out_, lhsT, rhs, start, stop):
                    return nc.tensor.matmul(out_, lhsT, rhs, start=start, stop=stop, skip_group_check=True)

                def mm3(outs, lh, ll, rh, rl, start, stop):
                    for i, o in enumerate(outs):
                        mm(o, lh, rh[i], start, False)
                    for i, o in enumerate(outs):
                        mm(o, lh, rl[i], False, False)
                    for i, o in enumerate(outs):
                        ins = mm(o, ll, rh[i], False, stop)
                    return ins

                def unit_cols(u, half, t, bank, n=512):
                    q = slice(t * 128, (t + 1) * 128)
                    for k in range(4):
                        kt = 4 * half + k
                        w = slice(512 * k, 512 * k + n)
                        ins = mm3([ps[:, bank, 0:n]], xhi[:, kt, q], xlo[:, kt, q],
                                  [whi[:, u % RING, w]], [wlo[:, u % RING, w]], kt == 0, kt == KT - 1)
                    return ins

                def unit_rows(u, xh, xl, kt0, t, bank, first, last, quarter=None):
                    q = slice(t * 128, (t + 1) * 128)
                    sl = u % RING
                    for k in range(2):
                        w = [slice(D * k + 512 * n, D * k + 512 * n + 512) for n in range(2)]
                        if quarter is not None and last and k == 1:
                            for n in range(2):
                                ins = mm3([ps[:, bank + n, :]], xh[:, kt0 + k, q], xl[:, kt0 + k, q],
                                          [whi[:, sl, w[n]]], [wlo[:, sl, w[n]]], False, True)
                                if 2 * t + n < 3:
                                    ins.then_inc(sem(f"br{quarter}_{2 * t + n}"), 1)
                            return ins
                        ins = mm3([ps[:, bank + n, :] for n in range(2)], xh[:, kt0 + k, q], xl[:, kt0 + k, q],
                                  [whi[:, sl, x] for x in w], [wlo[:, sl, x] for x in w],
                                  first and k == 0, last and k == 1)
                    return ins

                def done(ins):
                    ins.then_inc(sem("unit_used"), 1)

                def transpose(dst, src):
                    n = src.shape[0]
                    return nc.tensor.transpose(dst, src, ident[0:n, 0:n])

                def turn(e, t, src, waits, bank_waits):
                    for half in range(2):
                        after(waits[half])
                        if bank_waits:
                            after(bank_waits[half])
                        for k in range(4):
                            c = 512 * half + 128 * k
                            ins = transpose(two(TB[e][t][half], 4)[:, k, :], src[:, t, c:c + 128])
                        ins.then_inc(sem(f"xt{e}_{t}{half}"), 1)

                def turn_hg(e, t):
                    turn(e, t, hg, [f"hg{e}_{t}"] * 2, [f"xlo{e}_0{half}" for half in range(2)] if t else None)

                def ffn(b, f, e, extra=None):
                    def chunk(j, u, Uj=None):
                        split(u, Uj)
                        for t in range(TOK):
                            pe.wait_ge(sem(f"hact{f}_{t}"), j)
                            ins = unit_cols(u, 0, t, t)
                        done(ins)

                    def chunk_b(u, Uj=None):
                        split(u, Uj)
                        for t in range(TOK):
                            ins = unit_cols(u, 1, t, t)
                            if t == 0:
                                ins.then_inc(sem(f"gu{f}"), 1)
                        done(ins)

                    def hidden(j):
                        for t in range(TOK):
                            pe.wait_ge(sem(f"hact{f}_{t}"), j)
                        for k in range(2):
                            for t in range(TOK):
                                ins = transpose(two(2)[:, k, t * 128:(t + 1) * 128], hact[:, t, 128 * k:128 * k + 128])
                        ins.then_inc(sem(f"ht{f}"), 1)

                    def down(u, t, buf, first, last):
                        return unit_rows(u, yhi, ylo, 2 * buf, t, 4 + 2 * t, first, last)

                    for t in range(TOK):
                        for half in range(2):
                            after(f"xlo{e}_{t}{half}")
                            split(b + half)
                            ins = unit_cols(b + half, half, t, t)
                            if t == 1:
                                done(ins)
                            elif half == 1:
                                ins.then_inc(sem(f"gu{f}"), 1)
                    chunk(H0 + 1, b + 2)
                    hidden(H0 + 1)
                    chunk_b(b + 3)
                    pe.wait_ge(sem(f"htlo{f}"), H0 + 1)
                    split(b + 4)
                    for t in range(TOK):
                        ins = down(b + 4, t, 0, True, False)
                    done(ins)
                    with pe.Fori(2, NCH - 1) as j:
                        Hj = pe.snap(H0 + j)
                        Uj = pe.snap(U0 + j * 3)
                        chunk(Hj, b - 1, Uj)
                        hidden(Hj)
                        chunk_b(b, Uj)
                        pe.wait_ge(sem(f"htlo{f}"), Hj)
                        split(b + 1, Uj)
                        for t in range(TOK):
                            ins = down(b + 1, t, 0, False, False)
                        done(ins)
                    chunk(H0 + NCH - 1, b + 29)
                    hidden(H0 + NCH - 1)
                    chunk_b(b + 30)
                    pe.wait_ge(sem(f"htlo{f}"), H0 + NCH - 1)
                    split(b + 31)
                    down(b + 31, 0, 0, False, False)
                    hidden(H0 + NCH)
                    if extra:
                        extra()
                    done(down(b + 31, 1, 0, False, False))
                    pe.wait_ge(sem(f"htlo{f}"), H0 + NCH)
                    split(b + 32)
                    down(b + 32, 0, 1, False, True).then_inc(sem(f"f{0 if f == 1 else 2}_0"), 1)
                    done(down(b + 32, 1, 1, False, True))

                def scores(p):
                    c = PIECE[p]
                    v = ps_view(p)
                    q = slice(128 * c["qb"], 128 * c["qb"] + 128)
                    keys = slice(0, 128 * c["nk"])
                    for i, hh in enumerate(c["heads"]):
                        if p[0] == "A":
                            mm(v[:, i, :], qz[:, hh, q], kz[:, hh // 2, keys], True, False)
                            ins = mm(v[:, i, :], decL[:, hh, q], decR[:, keys], False, True)
                        else:
                            ins = mm(v[:, i, :], qz[:, hh, q], kz[:, hh // DG, keys], True, True)
                    ins.then_inc(sem(f"sc_{p}"), 1)

                def probs_t(p, r, wait):
                    c = PIECE[p]
                    after(f"pn_{p}")
                    if wait:
                        after(wait)
                    blocks = [(i, k) for i in range(len(c["heads"])) for k in range(c["nk"])][4 * r:4 * r + 4]
                    for n, (i, k) in enumerate(blocks):
                        ins = transpose(two(c["pt"][r], 4)[:, n, :], s_view(p)[:, i, 128 * k:128 * k + 128])
                    ins.then_inc(sem(f"tp_{p}_{r}"), 1)

                def values(p, rounds):
                    c = PIECE[p]
                    for r in range(rounds):
                        after(f"te_{p}_{r}")
                    for i, hh in enumerate(c["heads"]):
                        c0 = C_VA + hh * HD if p[0] == "A" else C_VD + (hh // DG) * HD
                        rows_ = slice(64 * (i % 2), 64 * (i % 2) + 64)
                        for k in range(c["nk"]):
                            ins = mm(ps[rows_, c["pv"], (i // 2) * 128:(i // 2) * 128 + 128],
                                     proj[:, k, c0:c0 + HD], PT[:, i * c["nk"] + k, :], k == 0, k == c["nk"] - 1)
                    ins.then_inc(sem(f"pv_{p}"), 1)

                def turn_cols(bank, cols, name):
                    for k, src in enumerate(cols):
                        for t in range(TOK):
                            ins = transpose(two(bank)[:, k, t * 128:(t + 1) * 128], src(t))
                    if name:
                        ins.then_inc(sem(name), 1)

                def pcol(c0):
                    return lambda t: proj[:, t, c0:c0 + 128]

                pe.wait_ge(sem("ident"), 1)
                for t in range(TOK):
                    turn_hg(0, t)
                ffn(U_FFN1, 1, 0)
                for t in range(TOK):
                    turn_hg(1, t)

                for u in range(U_HEAD, U_WO):
                    if u < U_GATE1:
                        c, half = (u - U_HEAD) // 2, (u - U_HEAD) % 2
                        n = min(512, HEAD_COLS - 512 * c)
                        split(u)
                        for t in range(TOK):
                            if c == 0:
                                after(f"xlo1_{t}{half}")
                            elif half == 0 and c >= 2:
                                after(f"proj{c - 2}_{t}")
                            ins = unit_cols(u, half, t, 2 * (c % 2) + t, n)
                            if t == 0 and half == 1:
                                ins.then_inc(sem(f"head{c}"), 1)
                        done(ins)
                    elif u < U_BR_B or U_GATE2 <= u < U_BR_D:
                        g, half = ((u - U_GATE1) // 2, (u - U_GATE1) % 2) if u < U_BR_B else \
                                  ((u - U_GATE2) // 2 + 4, (u - U_GATE2) % 2)
                        split(u)
                        for t in range(TOK):
                            if half == 0:
                                if g < 2:
                                    after(f"proj{4 + g}_{t}")
                                elif g in (4, 5):
                                    after(f"gb0_{2 * (g - 4) + t}")
                                else:
                                    pe.wait_ge(sem("gate_pre"), G0 + (2 * (g - 2) + t + 1))
                            ins = unit_cols(u, half, t, 2 * (g % 2) + t)
                            if t == 0 and half == 1:
                                ins.then_inc(sem(f"gate{g}"), 1)
                        done(ins)
                    elif u == U_BR_B:
                        split(u)
                        after("ybl")
                        pe.wait_ge(sem("gate_pre"), G0 + 8)
                        for t in range(TOK):
                            ins = unit_rows(u, yhi, ylo, Y[1], t, 2 * t, True, True, 0)
                        done(ins)
                    elif u == U_BR_A:
                        split(u)
                        for name in ("yl_A1", "yl_D0", "kD", "gT"):
                            after(name)
                        for t in range(TOK):
                            ins = unit_rows(u, yhi, ylo, Y[0], t, 4 + 2 * t, True, True, 1)
                        done(ins)
                    elif u < U_BR_C:
                        i = u - U_BR_D
                        split(u)
                        if i == 0:
                            after("yl_D1b")
                            pe.wait_ge(sem("gate_pre"), G0 + 16)
                        for t in range(TOK):
                            ins = unit_rows(u, yhi, ylo, Y[3] + 2 * i, t, 2 * t, i == 0, i == 1, 2)
                        done(ins)
                    else:
                        split(u)
                        after("ycl")
                        for t in range(TOK):
                            ins = unit_rows(u, yhi, ylo, Y[2], t, 4 + 2 * t, True, True, 3)
                        done(ins)

                    if u == 38:
                        for t in range(TOK):
                            after(f"proj0_{t}")
                        turn_cols(4, [pcol(C_QA), pcol(C_QA + 128)], None)
                        turn_cols(5, [pcol(C_KA), pcol(C_KA + 128)], "tA")
                    if u == 39:
                        pe.wait_ge(sem("small"), pe.snap(L * (16 * 7)) + 16 * 7)
                        after("lf")
                        for i in range(2):
                            mm(ps[:, 6, SEQ * i:SEQ * i + SEQ], lf[:, 0, i, :], cumU[:, :], True, False)
                            ins = mm(ps[:, 6, SEQ * i + 128:SEQ * i + SEQ], lf[:, 1, i, :], cumU[:, 0:128],
                                     False, True)
                        ins.then_inc(sem("cs"), 1)
                        for c in range(2):
                            ins = transpose(ps[:, 7, 35 * c:35 * c + 35], cwrow[:, 128 * c:128 * c + 128])
                        ins.then_inc(sem("tcw"), 1)
                    if u == 41:
                        for name in ("qA", "kA", "dec"):
                            after(name)
                        scores("A0")
                        scores("A1")
                    if u == 43:
                        probs_t("A0", 0, "cw")
                    if u == 44:
                        values("A0", 1)
                        probs_t("A1", 0, None)
                        probs_t("A1", 1, None)
                    if u == 45:
                        values("A1", 2)
                    if u == 46:
                        after("cgxb")
                        after("yl_A0")
                        turn_cols(4, [pcol(C_XB), pcol(C_XB + 128)], None)
                        turn_cols(5, [pcol(C_BG), pcol(C_BG + 128)], "tB")
                    if u == 47:
                        after("yl_A1")
                        turn_cols(6, [pcol(C_QD), pcol(C_QD + 128)], None)
                        turn_cols(7, [pcol(C_QD + 256), pcol(C_QD + 384)], "tD")
                    if u == 48:
                        after("uT")
                        after("kdup")
                        turn_cols(4, [lambda t, g=g: kdup[:, t, g].rearrange("p r d -> p (r d)") for g in range(2)],
                                  "tDk")
                        after("bgT")
                        after("glu")
                        turn_cols(5, [pcol(C_CA), pcol(C_CA + 128)], "tC")
                    if u == 49:
                        after("qD1")
                        after("kD")
                        scores("D0")
                    if u == 51:
                        after("gT")
                        probs_t("D0", 0, None)
                        probs_t("D0", 1, None)
                    if u == 52:
                        values("D0", 2)
                    if u == 55:
                        after("gb1_0")
                        after("gb1_1")
                        scores("D1a")
                    if u == 56:
                        after("gb1_2")
                        after("gb1_3")
                        scores("D1b")
                    if u == 58:
                        probs_t("D1a", 0, None)
                        probs_t("D1a", 1, None)
                    if u == 59:
                        values("D1a", 2)
                    if u == 60:
                        probs_t("D1b", 0, None)
                        probs_t("D1b", 1, None)
                    if u == 61:
                        values("D1b", 2)
                        for c in range(2):
                            pe.wait_ge(sem(f"cc{c}"), pe.snap(L * KC) + KC)
                        for t in range(TOK):
                            for c in range(2):
                                ins = transpose(two(6)[:, t, 128 * c:128 * c + 128],
                                                acc[:, c, t * 128:(t + 1) * 128])
                        ins.then_inc(sem("t5"), 1)
                    if u == 63:
                        after("lnm")
                        turn_cols(7, [pcol(C_CA), pcol(C_CA + 128)], "t6")

                for t in range(TOK):
                    turn(2, t, hg, [f"merged_{2 * t}", f"merged_{2 * t + 1}"], None)
                for i in range(4):
                    u = U_WO + i
                    split(u)
                    for t in range(TOK):
                        if i == 0:
                            after(f"xlo2_{t}1")
                        ins = unit_rows(u, xhi, xlo, 2 * i, t, FB[1] + 2 * t, i == 0, i == 3)
                        if i == 3 and t == 0:
                            ins.then_inc(sem("f1_0"), 1)
                    done(ins)
                for t in range(TOK):
                    turn_hg(3, t)

                def p_turn():
                    pe.wait_ge(sem("p_in"), pe.snap(L * 16) + 16)
                    turn_cols(3, [lambda t: pin[:, t, 0:128], lambda t: pin[:, t, 128:256]], "tp")

                ffn(U_FFN2, 2, 3, p_turn)
                split(U_PLE)
                after("pl")
                for t in range(TOK):
                    if t == 1:
                        after("n2_0")
                    ins = unit_rows(U_PLE, yhi, ylo, 4, t, PB[t], True, True)
                    if t == 0:
                        ins.then_inc(sem("pd"), 1)
                    else:
                        done(ins)
                    turn_hg(4, t)
                for i in range(4):
                    u = U_PGATE + i
                    split(u)
                    for t in range(TOK):
                        if i == 0:
                            after(f"n2_1")
                            after(f"xlo4_{t}1")
                        ins = unit_rows(u, xhi, xlo, 2 * i, t, GB[t], i == 0, i == 3)
                        if i == 3 and t == 0:
                            ins.then_inc(sem("gd"), 1)
                    done(ins)


INPUTS = ["x", "p", "ffn1_norm_pre", "ffn1_w_gu", "ffn1_w_down", "ffn1_norm_post", "mix_norm_pre", "w_in",
          "b_forget", "b_gate", "conv_short", "conv_dw", "conv_dw_bias", "conv_ln_gain", "conv_ln_bias",
          "attn_sinks", "rel_bias", "w_br_a", "w_br_b", "w_br_c", "w_br_d", "w_o", "mix_norm_post",
          "ffn2_norm_pre", "ffn2_w_gu", "ffn2_w_down", "ffn2_norm_post", "ple_norm_gate", "w_ple_gate",
          "w_ple", "ple_norm_post"]


def kernel(**inputs):
    import concourse.bacc as bacc
    from concourse.bass_utils import run_bass_kernel_spmd

    nc = bacc.Bacc("TRN2", target_bir_lowering=False, num_devices=1)
    arrays, aps = {}, {}
    for name in INPUTS:
        a = np.ascontiguousarray(inputs[name])
        arrays[f"in_{name}"] = a
        aps[name] = nc.dram_tensor(f"in_{name}", a.shape, mybir.dt.from_np(a.dtype), kind="ExternalInput").ap()
    out = nc.dram_tensor("out_0", (1, SEQ, D), F32, kind="ExternalOutput").ap()
    build(nc, aps, out)
    r = run_bass_kernel_spmd(nc, [arrays], core_ids=[0])
    return r.results[0]["out_0"]
```

```python
import math
from contextlib import ExitStack

import numpy as np

import concourse.bass as bass
from concourse import mybir

F32 = mybir.dt.float32
F32R = mybir.dt.float32r
ALU = mybir.AluOpType
ACT = mybir.ActivationFunctionType
AX = mybir.AxisListType

D = 1024
SEQ = 256
DEPTH = 2
DFF = 2816
TOK = SEQ // 128
KT = D // 128
HD = 64
AH, DH, DG = 4, 8, 4
CW = 256
KC, KS = 31, 3
EPS = 1e-6
NEG = -1e30
BUCKETS, MAXDIST, WINDOW = 32, 128, 128
QSCALE = HD ** -0.5

C_QA, C_KA, C_VA, C_F = 0, 256, 512, 768
C_BG, C_CG, C_XB = 772, 1028, 1284
C_CA, C_CB = 1540, 1796
C_QD, C_KD, C_VD = 2052, 2564, 2692
HEAD_COLS = 2820
HEAD_CHUNKS = 6

UNIT = 2048
NCH = DFF // 256
FFN_UNITS = 3 * NCH
U_FFN1 = 0
U_HEAD = U_FFN1 + FFN_UNITS
U_GATE1 = U_HEAD + 2 * HEAD_CHUNKS
U_BR_B = U_GATE1 + 8
U_BR_A = U_BR_B + 1
U_GATE2 = U_BR_A + 1
U_BR_D = U_GATE2 + 8
U_BR_C = U_BR_D + 2
U_WO = U_BR_C + 1
U_FFN2 = U_WO + 4
U_PLE = U_FFN2 + FFN_UNITS
U_PGATE = U_PLE + 1
UNITS = U_PGATE + 4
RING = 3
assert UNITS % RING == 0
UNIT_INCS = 32
GATE_ORDER = [1, 0, 3, 2]


def bucket(dist):
    exact = BUCKETS // 2
    if dist < exact:
        return dist
    return min(exact + int(math.log(dist / exact) / math.log(MAXDIST / exact) * (BUCKETS - exact)), BUCKETS - 1)


TAPS = [4, 5, 2, 2, 4, 4, 2, 2, 3, 3]
assert sum(TAPS) == KC
PIECES = ["A0", "A1", "D0", "D1a", "D1b"]
ROUNDS = {"A0": 1, "A1": 2, "D0": 2, "D1a": 2, "D1b": 2}
NORMS = [3, 0, 4, 8, 1, 5, 2, 6, 7]


def gate_chunk(u):
    for first, g in ((U_GATE1, 0), (U_GATE2, 4)):
        if first <= u < first + 8 and (u - first) % 2:
            return g + (u - first) // 2
    return None


def event_families():
    turns = [f"{e}_{t}{half}" for e in range(5) for t in range(TOK) for half in range(2)]
    norms = [f"{n}_{t}" for n in NORMS for t in range(TOK)]
    quarters = [f"{i}_{q}" for i in range(4) for q in range(4)]
    rounds = [f"{p}_{r}" for p in PIECES for r in range(ROUNDS[p])]
    ends = [f"{s}_{t}" for s in range(3) for t in range(TOK)]
    fam = {
        "xt": turns, "xhi": turns, "xlo": turns,
        "ms": norms, "ve": norms, "rs": norms,
        "br": [x for x in quarters if x[-1] != "3"], "gb": quarters,
        "add": [f"{i}_{q}" for i in (1, 2) for q in range(4)],
        "merged_": [str(q) for q in range(4)],
        "proj": [f"{c}_{t}" for c in range(HEAD_CHUNKS) for t in range(TOK)],
        "head": [str(c) for c in range(HEAD_CHUNKS)],
        "gate": [str(g) for g in range(8)],
        "h": ends, "n": ends, "tm": ends, "tg": ends, "hp": ends,
        "hg": [f"{e}_{t}{half}" for e in (0, 1, 3, 4) for t in range(TOK) for half in range(2)],
        "tp_": rounds, "te_": rounds,
    }
    for kind in ("sc_", "sm_", "ma_", "nm_", "ex_", "rc_", "pn_", "pv_", "yh_", "yl_"):
        fam[kind] = PIECES
    for kind in ("mb_", "sx_", "sa_"):
        fam[kind] = PIECES[2:]
    fam["gg"] = ["0", "1", "2"]
    places = {kind + x: (kind, n + 1, len(xs)) for kind, xs in fam.items() for n, x in enumerate(xs)}
    for chain, names in {
        "forget_terms": ["zabs", "zexp", "zln"],
        "layer_norm": ["lnsum", "lnmean", "xc0", "xc1", "lng0", "lng1"],
        "branch_products": ["cgxb", "glu", "lny", "lnm"],
        "queries": ["qA", "qD0", "qD1"],
        "keys": ["kA", "kD"],
        "gains_halved": ["gh0", "gh2"],
        "cb_copies": ["uT", "bgT"],
    }.items():
        places.update({x: (chain, n + 1, len(names)) for n, x in enumerate(names)})
    return places


class Events:

    def __init__(self, nc, stack):
        self.nc, self.stack, self.sems, self.places = nc, stack, {}, event_families()

    def sem(self, name):
        name = self.places[name][0] if name in self.places else name
        if name not in self.sems:
            self.sems[name] = self.stack.enter_context(self.nc.semaphore(name))
        return self.sems[name]

    def wait(self, eng, name, L, L1):
        eng.wait_ge(self.sem(name), self.count(eng, name, L, L1))

    def count(self, eng, name, L, L1):
        if name not in self.places:
            return L1
        _, place, n = self.places[name]
        return eng.snap(L * n) + place


def build(nc, A, out):
    stack = ExitStack()
    with stack:
        ev = Events(nc, stack)
        sem = ev.sem

        def sb(name, shape, dt=F32):
            return stack.enter_context(nc.sbuf_tensor(name, shape, dt))

        raw = sb("raw", [128, RING, UNIT])
        whi = sb("whi", [128, RING, UNIT], F32R)
        wlo = sb("wlo", [128, RING, UNIT], F32R)
        h = sb("h", [128, TOK, D])
        hg = sb("hg", [128, TOK, D])
        xhi = sb("xhi", [128, KT, SEQ], F32R)
        xlo = sb("xlo", [128, KT, SEQ], F32R)
        yhi = sb("yhi", [128, 8, SEQ], F32R)
        ylo = sb("ylo", [128, 8, SEQ], F32R)
        proj = sb("proj", [128, TOK, HEAD_COLS])
        gates = sb("gates", [128, TOK, 2 * D])
        gbias = sb("gbias", [128, 2, 512])
        gpre = sb("gpre", [128, D])
        gpost = sb("gpost", [128, D])
        qz = sb("qz", [128, DH, SEQ])
        kz = sb("kz", [128, 2, SEQ])
        S = sb("S", [128, 2, 1024])
        PT = sb("PT", [128, 8, 128])
        cumU = sb("cumU", [128, SEQ])
        maskA = sb("maskA", [128, SEQ])
        bandD = sb("bandD", [128, DH, SEQ])
        ident = sb("ident", [128, 128])
        lf = sb("lf", [128, TOK, 2, 128])
        cstc = sb("cstc", [128, 8])
        cwT = sb("cwT", [128, 2, 35])
        lnp = sb("lnp", [128, 2, CW])
        bfs = sb("bfs", [128, AH])
        snk = sb("snk", [128, DH])
        st = sb("st", [128, 160])
        epsc = sb("epsc", [128, 12])
        relT = sb("relT", [DH, BUCKETS])

        acc = proj[:, :, C_QA:C_QA + SEQ]
        bgT = proj[:, :, C_KA:C_KA + SEQ]
        upad = proj[:, :, C_BG:C_BG + SEQ + KS - 1]
        gpad = proj[:, :, C_QD:C_QD + SEQ + KC - 1]
        decL = hg[:, 1, :].rearrange("p (h q) -> p h q", h=AH)
        decR = PT[:, 2:4, :].rearrange("p a b -> p (a b)")
        cwrow = PT[0:35, 0:2, :].rearrange("p a b -> p (a b)")
        pin = proj[:, :, 0:CW]
        tmp = gates[:, :, 0:D]
        hpre = gates[:, :, D:2 * D]
        silu = S[:, 0, 0:512].rearrange("p (t n) -> p t n", t=TOK)
        hact = S[:, 1, 0:512].rearrange("p (t n) -> p t n", t=TOK)
        kdup = hg[:, 0, 0:512].rearrange("p (t g r d) -> p t g r d", t=TOK, g=2, r=2)
        relrow = bandD[0:DH, 0:2, :].rearrange("p a b -> p (a b)")
        relscr = nc.dram_tensor("rel_scratch", (DH, 128, 512), F32, kind="Internal").ap()

        ps = stack.enter_context(nc.psum_tensor("ps", [128, 8, 512], F32))

        def ms(s, t): return st[:, 2 * s + t:2 * s + t + 1]
        def rs(s, t): return st[:, 32 + 2 * s + t:33 + 2 * s + t]
        def ve(s, t): return st[:, 144 + t:145 + t]
        N_PRE = {0: 3, 1: 4, 3: 5, 4: 6}
        N_PLE = 7
        N_LN = 8
        def mx(p): i = PIECES.index(p); return st[:, 64 + 16 * i:64 + 16 * i + 8]
        def sums(p): i = PIECES.index(p); return st[:, 72 + 16 * i:72 + 16 * i + 8]
        sexp = sb("sexp", [128, 2, 8])

        PIECE = {
            "A0": dict(heads=[0, 1, 2, 3], qb=0, nk=1, bank=4, buf=0, pt=[7], pv=4),
            "A1": dict(heads=[0, 1, 2, 3], qb=1, nk=2, bank=5, buf=1, pt=[7, 5], pv=6),
            "D0": dict(heads=list(range(8)), qb=0, nk=1, bank=6, buf=0, pt=[4, 5], pv=6),
            "D1a": dict(heads=[0, 1, 2, 3], qb=1, nk=2, bank=4, buf=1, pt=[4, 5], pv=4),
            "D1b": dict(heads=[4, 5, 6, 7], qb=1, nk=2, bank=6, buf=0, pt=[6, 7], pv=5),
        }

        def s_view(p):
            c = PIECE[p]
            n = len(c["heads"])
            return S[:, c["buf"], 0:n * c["nk"] * 128].rearrange("p (h k) -> p h k", h=n)

        def ps_view(p):
            c = PIECE[p]
            n = len(c["heads"])
            w = n * c["nk"] * 128
            flat = ps[:, c["bank"]:c["bank"] + (w + 511) // 512, :].rearrange("p a b -> p (a b)")
            return flat[:, 0:w].rearrange("p (h k) -> p h k", h=n)

        zt = sb("zt", [128, 2, TOK, AH])
        PB = [0, 4]
        GB = [6, 2]

        def lnx(t): return proj[:, t, C_CA:C_CA + CW]
        def lnj(t): return proj[:, t, C_CB:C_CB + CW]
        lnx2 = proj[:, :, C_CA:C_CA + CW]
        lnj2 = proj[:, :, C_CB:C_CB + CW]

        def yslice(p):
            if p[0] == "A":
                return Y[0], 2, 128 * PIECE[p]["qb"]
            return Y[3] + (2 if p == "D1b" else 0), (4 if p == "D0" else 2), 128 * PIECE[p]["qb"]

        def two(bank, k=2):
            return ps[:, bank, :].rearrange("p (k n) -> p k n", k=k)

        def wide(bank):
            return ps[:, bank:bank + 2, :].rearrange("p a b -> p (a b)")

        Y = {1: 0, 0: 2, 2: 0, 3: 4}

        TB = {0: [[4, 5], [4, 5]], 1: [[2, 3], [2, 3]], 2: [[0, 1], [2, 3]], 3: [[2, 3], [2, 3]], 4: [[2, 3], [2, 3]]}
        FB = {0: 4, 1: 4, 2: 4}

        def gate_bias(eng, L, g):
            c0 = GATE_ORDER[g // 2] * D + (g % 2) * 512
            for c in (256, 0):
                src = A["b_gate"][bass.ds(L, 1), c0 + c:c0 + c + 256]
                eng.dma_start(gbias[:, g % 2, c:c + 256], src.to_broadcast([128, 256]))\
                   .then_inc(sem(f"gbias{g % 2}"), 16)

        block = stack.enter_context(nc.Block())

        @block.sync
        def _(sp):
            def bc(dst, src, name):
                return sp.dma_start(dst, src.to_broadcast([128, dst.shape[-1]])).then_inc(sem(name), 16)

            for t in range(TOK):
                sp.dma_start(h[:, t, :], A["x"][0, t * 128:(t + 1) * 128, :]).then_inc(sem("x_in"), 16)
            with nc.allow_non_contiguous_dma(reason="32 x 8 table, once"):
                sp.dma_start(relT[:, :], A["rel_bias"].rearrange("b h -> h b")).then_inc(sem("rel_in"), 16)

            with sp.Fori(0, DEPTH) as L:
                L1 = sp.snap(L + 1)
                U0 = sp.snap(L * UNITS)

                def free(u, base=None):
                    sp.wait_ge(sem("lo_ready"), (U0 if base is None else base) + (u + 1))

                def load(u, d0, s0, d1, s1, base=None):
                    free(u, base)
                    sp.dma_start(d0, s0).then_inc(sem(f"raw{u % RING}"), 16)
                    sp.dma_start(d1, s1).then_inc(sem(f"raw{u % RING}"), 16)

                def slot(u, k):
                    return raw[:, u % RING, :].rearrange("p (k n) -> p k n", k=k)

                def cols(u, w, r0, c0, n=512):
                    v = slot(u, 4)
                    load(u, v[:, 0:2, 0:n], w[L, r0:r0 + 256, c0:c0 + n].rearrange("(k p) n -> p k n", p=128),
                         v[:, 2:4, 0:n], w[L, r0 + 256:r0 + 512, c0:c0 + n].rearrange("(k p) n -> p k n", p=128))

                def rows(u, w, r0):
                    v = slot(u, 2)
                    load(u, v[:, 0, :], w[L, r0:r0 + 128, :], v[:, 1, :], w[L, r0 + 128:r0 + 256, :])

                def gate_up(u, w, half, c0, base=None):
                    v = slot(u, 4)
                    r0 = half * 512
                    load(u, v[:, :, 0:256],
                         w[L, r0:r0 + 512, bass.ds(c0, 256)].rearrange("(k p) n -> p k n", p=128),
                         v[:, :, 256:512],
                         w[L, r0:r0 + 512, bass.ds(c0 + DFF, 256)].rearrange("(k p) n -> p k n", p=128), base)

                def down(u, w, r0, base=None):
                    v = slot(u, 2)
                    load(u, v[:, 0, :], w[L, bass.ds(r0, 128), :], v[:, 1, :], w[L, bass.ds(r0 + 128, 128), :], base)

                def ffn(b, f, extra):
                    wg, wd = A[f"ffn{f}_w_gu"], A[f"ffn{f}_w_down"]
                    extra(0)
                    gate_up(b, wg, 0, 0)
                    gate_up(b + 1, wg, 1, 0)
                    gate_up(b + 2, wg, 0, 256)
                    gate_up(b + 3, wg, 1, 256)
                    down(b + 4, wd, 0)
                    extra(1)
                    with sp.Fori(2, NCH) as j:
                        Uj = sp.snap(U0 + j * 3)
                        c0 = sp.snap(j * 256)
                        r0 = sp.snap(j * 256 - 256)
                        gate_up(b - 1, wg, 0, c0, Uj)
                        gate_up(b, wg, 1, c0, Uj)
                        down(b + 1, wd, r0, Uj)
                    down(b + FFN_UNITS - 1, wd, DFF - 256)

                def small(dst, src):
                    sp.dma_start(dst, src).then_inc(sem("small"), 16)

                def extra1(i):
                    if i == 0:
                        bc(gpre[:, :], A["ffn1_norm_pre"][bass.ds(L, 1), :], "gpre0")
                        return
                    bc(gpost[:, :], A["ffn1_norm_post"][bass.ds(L, 1), :], "gpost0")
                    sp.wait_ge(sem("relscr"), 16)
                    sp.dma_start(bandD[:, :, :], bass.AP(relscr.tensor, 127, [[511, 128], [128 * 512, DH], [1, SEQ]]))\
                      .then_inc(sem("band"), 16)
                    small(cwrow[0:KC, :], A["conv_dw"][L, :, :])
                    small(cwrow[KC:KC + KS, :], A["conv_short"][L, :, :])
                    small(cwrow[34:35, :], A["conv_dw_bias"][bass.ds(L, 1), :])
                    small(lnp[:, 0, :], A["conv_ln_gain"][bass.ds(L, 1), :].to_broadcast([128, CW]))
                    small(lnp[:, 1, :], A["conv_ln_bias"][bass.ds(L, 1), :].to_broadcast([128, CW]))
                    small(bfs[:, :], A["b_forget"][bass.ds(L, 1), :].to_broadcast([128, AH]))
                    small(snk[:, :], A["attn_sinks"][bass.ds(L, 1), :].to_broadcast([128, DH]))
                    ev.wait(sp, "hg0_11", L, L1)
                    bc(gpre[:, :], A["mix_norm_pre"][bass.ds(L, 1), :], "gpre1")

                ffn(U_FFN1, 1, extra1)

                for c in range(HEAD_CHUNKS):
                    n = min(512, HEAD_COLS - 512 * c)
                    cols(U_HEAD + 2 * c, A["w_in"], 0, 512 * c, n)
                    cols(U_HEAD + 2 * c + 1, A["w_in"], 512, 512 * c, n)
                    if c == 2:
                        ev.wait(sp, "h0_1", L, L1)
                        bc(gpost[:, :], A["mix_norm_post"][bass.ds(L, 1), :], "gpost1")
                        bc(gpre[:, :], A["ffn2_norm_pre"][bass.ds(L, 1), :], "gpre3")
                        gate_bias(sp, L, 0)
                        gate_bias(sp, L, 1)
                for g in range(8):
                    u = (U_GATE1 if g < 4 else U_GATE2 - 8) + 2 * g
                    c0 = HEAD_COLS + GATE_ORDER[g // 2] * D + (g % 2) * 512
                    cols(u, A["w_in"], 0, c0)
                    cols(u + 1, A["w_in"], 512, c0)
                    if g == 3:
                        rows(U_BR_B, A["w_br_b"], 0)
                        rows(U_BR_A, A["w_br_a"], 0)
                rows(U_BR_D, A["w_br_d"], 0)
                rows(U_BR_D + 1, A["w_br_d"], 256)
                rows(U_BR_C, A["w_br_c"], 0)
                for i in range(4):
                    rows(U_WO + i, A["w_o"], 256 * i)

                def extra2(i):
                    if i == 1:
                        ev.wait(sp, "h1_1", L, L1)
                        bc(gpost[:, :], A["ffn2_norm_post"][bass.ds(L, 1), :], "gpost2")
                        bc(gpre[:, :], A["ple_norm_gate"][bass.ds(L, 1), :], "gpre4")
                        sp.dma_start(pin, A["p"][L, 0, :, :].rearrange("(t p) n -> p t n", p=128))\
                          .then_inc(sem("p_in"), 16)

                ffn(U_FFN2, 2, extra2)
                rows(U_PLE, A["w_ple"], 0)
                for i in range(4):
                    rows(U_PGATE + i, A["w_ple_gate"], 256 * i)
                ev.wait(sp, "h2_1", L, L1)
                bc(gpost[:, :], A["ple_norm_post"][bass.ds(L, 1), :], "gpost3")

            for t in range(TOK):
                sp.wait_ge(sem(f"h3_{t}"), DEPTH + 1)
                sp.dma_start(out[0, t * 128:(t + 1) * 128, :], h[:, t, :]).then_inc(sem("out"), 16)
            sp.wait_ge(sem("out"), 16 * TOK)

        @block.scalar
        def _(act):
            with act.Fori(0, DEPTH) as L:
                L1 = act.snap(L + 1)
                U0 = act.snap(L * UNITS)
                R0 = act.snap(L * (UNITS // RING * UNIT_INCS))
                H0 = act.snap(L * NCH)

                def after(name):
                    ev.wait(act, name, L, L1)

                def used(u):
                    act.wait_ge(sem("unit_used"), U0 + (u + 1 + RING))

                def hi(u, n=512):
                    act.wait_ge(sem(f"raw{u % RING}"), R0 + UNIT_INCS * (u // RING + 1))
                    act.wait_ge(sem("unit_used"), U0 + (u + 1))
                    s, d = (v[:, u % RING, :].rearrange("p (k n) -> p k n", k=4)[:, :, 0:n] for v in (raw, whi))
                    act.activation(d, s, ACT.Copy).then_inc(sem("hi_ready"), 1)

                def hi_j(u, Uj, Rj):
                    act.wait_ge(sem(f"raw{u % RING}"), Rj + UNIT_INCS * (u // RING + 1))
                    act.wait_ge(sem("unit_used"), Uj + (u + 1))
                    act.activation(whi[:, u % RING, :], raw[:, u % RING, :], ACT.Copy).then_inc(sem("hi_ready"), 1)

                def mean_square(dst, src, width, junk, name):
                    act.activation(junk, src, ACT.Square, scale=width ** -0.5, accum_out=dst)\
                       .then_inc(sem(name), 1)

                def copy(dst, src, wait, name, scale=1.0):
                    after(wait)
                    act.activation(dst, src, ACT.Copy, scale=scale).then_inc(sem(name), 1)

                def transposed(e, t):
                    for half in range(2):
                        copy(xhi[:, 4 * half:4 * half + 4, t * 128:(t + 1) * 128], two(TB[e][t][half], 4),
                             f"xt{e}_{t}{half}", f"xhi{e}_{t}{half}")

                def pre_stats(e, t, hname):
                    after(f"{hname}_{t}")
                    mean_square(ms(N_PRE[e], t), h[:, t, :], D, gates[:, t, 0:D], f"ms{N_PRE[e]}_{t}")

                def boundary(s, e, nxt):
                    after(f"f{s}_0")
                    mean_square(ms(s, 0), wide(FB[s]), D, hg[:, 0, :], f"ms{s}_0")
                    hi(nxt + 1)
                    transposed(e, 0)
                    used(nxt - 1)
                    mean_square(ms(s, 1), wide(FB[s] + 2), D, hg[:, 1, :], f"ms{s}_1")
                    for t in range(TOK):
                        after(f"n{s}_{t}")
                        act.activation(tmp[:, t, :], wide(FB[s] + 2 * t), ACT.Copy, scale=rs(s, t))\
                           .then_inc(sem(f"tm{s}_{t}"), 1)
                    transposed(e, 1)
                    hi(nxt + 2)
                    pre_stats(e, 0, f"h{s}")

                def ffn(b, f, e, h_before, extra=None):
                    def gate(tok, j, u=None, Uj=None):
                        if tok == 0:
                            act.wait_ge(sem(f"gu{f}"), j)
                        else:
                            act.wait_ge(sem("unit_used"), (U0 if Uj is None else Uj) + (u + 1 + RING))
                        act.activation(silu[:, tok, :], ps[:, tok, 0:256], ACT.Silu,
                                       scale=rs(N_PRE[e], tok)).then_inc(sem(f"silu{f}_{tok}"), 1)

                    def hidden(j, buf):
                        act.wait_ge(sem(f"ht{f}"), j)
                        act.activation(yhi[:, 2 * buf:2 * buf + 2, :], two(2), ACT.Copy).then_inc(sem(f"hthi{f}"), 1)

                    for t in range(TOK):
                        after(f"rs{N_PRE[e]}_{t}")
                        gate(t, H0 + 1, b + 1)
                        if t == 0:
                            hi(b + 3)
                            if h_before:
                                pre_stats(e, 1, h_before)
                    hi(b + 4)
                    hidden(H0 + 1, 0)
                    hi(b + 5)
                    for t in range(TOK):
                        gate(t, H0 + 2, b + 3)
                    hi(b + 6)
                    hi(b + 7)
                    with act.Fori(2, NCH - 1) as j:
                        Hj = act.snap(H0 + j)
                        Uj = act.snap(U0 + j * 3)
                        Rj = act.snap(R0 + j * UNIT_INCS)
                        hidden(Hj, 0)
                        hi_j(b + 2, Uj, Rj)
                        for t in range(TOK):
                            gate(t, Hj + 1, b, Uj)
                        hi_j(b + 3, Uj, Rj)
                        hi_j(b + 4, Uj, Rj)
                    hidden(H0 + NCH - 1, 0)
                    if extra:
                        extra()
                    hi(b + 32)
                    for t in range(TOK):
                        gate(t, H0 + NCH, b + 30)
                    hidden(H0 + NCH, 1)
                    hi(b + 33)

                def exps(p):
                    c = PIECE[p]
                    v = s_view(p)
                    n = len(c["heads"])
                    after(f"nm_{p}")
                    for i in range(n):
                        ins = act.activation(v[:, i, :], v[:, i, :], ACT.Exp, bias=mx(p)[:, i:i + 1],
                                             accum_out=sums(p)[:, i:i + 1])
                    ins.then_inc(sem(f"ex_{p}"), 1)
                    if p[0] == "D":
                        act.activation(sexp[:, c["buf"], 0:n], sexp[:, c["buf"], 0:n], ACT.Exp)\
                           .then_inc(sem(f"sx_{p}"), 1)

                def probs_t(p, r):
                    n = min(4, len(PIECE[p]["heads"]) * PIECE[p]["nk"] - 4 * r)
                    copy(PT[:, 4 * r:4 * r + n, :], two(PIECE[p]["pt"][r], 4)[:, 0:n, :], f"tp_{p}_{r}", f"te_{p}_{r}")

                def y_hi(p):
                    y0, n, q = yslice(p)
                    copy(yhi[:, y0:y0 + n, q:q + 128],
                         ps[:, PIECE[p]["pv"], 0:n * 128].rearrange("p (k n) -> p k n", k=n), f"pv_{p}", f"yh_{p}")

                def queries(bank, h0, name):
                    v = two(bank)
                    act.activation(qz[0:64, h0:h0 + 4:2, :], v[0:64], ACT.Copy, scale=QSCALE)
                    act.activation(qz[64:128, h0 + 1:h0 + 4:2, :], v[64:128], ACT.Copy, scale=QSCALE)\
                       .then_inc(sem(name), 1)

                def sigmoid_gates(first_chunk, i):
                    act.wait_ge(sem("gate_pre"), act.snap(L * 16) + (2 * first_chunk + 4))
                    act.activation(gates[:, :, (i % 2) * D:(i % 2 + 1) * D], gates[:, :, (i % 2) * D:(i % 2 + 1) * D],
                                   ACT.Sigmoid).then_inc(sem(f"sig{i}"), 1)

                act.wait_ge(sem("c_eps"), 1)
                act.activation(sexp[:, 0, 0:4], epsc[:, 0:4], ACT.Copy)
                hi(0)
                transposed(0, 0)
                hi(1)
                for t in range(TOK):
                    pre_stats(0, t, "h3")
                transposed(0, 1)
                hi(2)
                ffn(U_FFN1, 1, 0, None)
                boundary(0, 1, U_HEAD)
                pre_stats(1, 1, "h0")

                for u in range(U_HEAD, U_WO + 4):
                    if u == 44:
                        probs_t("A0", 0)
                    if u == 59:
                        probs_t("D1a", 0)
                        probs_t("D1a", 1)
                    if u == 53:
                        y_hi("D0")
                    if U_HEAD < u < U_WO + 3:
                        hi(u + 2, HEAD_COLS - 5 * 512 if u + 2 in (U_GATE1 - 2, U_GATE1 - 1) else 512)
                    if u == 42:
                        exps("A0")
                        exps("A1")
                    if U_HEAD <= u < U_GATE1 and (u - U_HEAD) % 2:
                        c = (u - U_HEAD) // 2
                        n = min(512, HEAD_COLS - 512 * c)
                        for t in range(TOK):
                            after(f"rs{N_PRE[1]}_{t}")
                            after(f"head{c}") if t == 0 else used(u)
                            act.activation(proj[:, t, 512 * c:512 * c + n], ps[:, 2 * (c % 2) + t, 0:n],
                                           ACT.Copy, scale=rs(N_PRE[1], t)).then_inc(sem(f"proj{c}_{t}"), 1)
                    g = gate_chunk(u - 2)
                    if g is not None and g < 6:
                        act.wait_ge(sem("gate_pre"), act.snap(L * 16) + (2 * g + 2))
                        gate_bias(act, L, g + 2)
                    if u == 37:
                        after("z")
                        act.activation(zt[:, 1], zt[:, 0], ACT.Abs).then_inc(sem("zabs"), 1)
                        after("zabs")
                        act.activation(zt[:, 1], zt[:, 1], ACT.Exp, scale=-1.0).then_inc(sem("zexp"), 1)
                        after("zexp")
                        act.activation(zt[:, 1], zt[:, 1], ACT.Ln, bias=1.0).then_inc(sem("zln"), 1)
                    if u == 39:
                        after("tA")
                        queries(4, 0, "qA")
                        copy(kz[:, :, :], two(5), "tA", "kA")
                    if u == 45:
                        y_hi("A0")
                        probs_t("A1", 0)
                        probs_t("A1", 1)
                    if u == 46:
                        y_hi("A1")
                        for t in range(TOK):
                            after(f"proj4_{t}")
                        act.activation(lnj2, lnj2, ACT.Sigmoid).then_inc(sem("csig"), 1)
                        for t in range(TOK):
                            after(f"proj5_{t}")
                        for t in range(TOK):
                            ins = act.activation(kdup[:, t], proj[:, t, C_KD:C_KD + 128]
                                                 .rearrange("p (g d) -> p g d", g=2).unsqueeze(2)
                                                 .to_broadcast([128, 2, 2, HD]), ACT.Copy)
                        ins.then_inc(sem("kdup"), 1)
                    if u == 47:
                        copy(upad[:, :, KS - 1:], two(4), "tB", "uT")
                        copy(bgT[:, :, :], two(5), "tB", "bgT")
                    if u == 48:
                        after("tD")
                        queries(6, 0, "qD0")
                        queries(7, 4, "qD1")
                    if u == 49:
                        copy(kz[:, :, :], two(4), "tDk", "kD")
                        copy(gpad[:, :, KC - 1:], two(5), "tC", "gT")
                    if u == 50:
                        copy(yhi[:, Y[1]:Y[1] + 2, :], acc[:, :, :], "yb", "ybh")
                        exps("D0")
                    if u == 52:
                        probs_t("D0", 0)
                        probs_t("D0", 1)
                        for i in range(2):
                            sigmoid_gates(2 * i, i)
                    if u == 56:
                        exps("D1a")
                    if u == 58:
                        exps("D1b")
                    if u == 60:
                        y_hi("D1a")
                        sigmoid_gates(4, 2)
                    if u == 61:
                        probs_t("D1b", 0)
                        probs_t("D1b", 1)
                    if u == 62:
                        y_hi("D1b")
                        for t in range(TOK):
                            after(f"xc{t}")
                            mean_square(ms(N_LN, t), lnx(t), CW, lnj(t), f"ms{N_LN}_{t}")
                        sigmoid_gates(6, 3)
                    if u == 63:
                        after("lny")
                        act.activation(lnj2, lnx2, ACT.Sigmoid).then_inc(sem("lnsig"), 1)
                    if u == 64:
                        copy(yhi[:, Y[2]:Y[2] + 2, :], two(7), "t6", "ych")
                    if u == 65:
                        for t in range(TOK):
                            transposed(2, t)
                boundary(1, 3, U_FFN2)

                ffn(U_FFN2, 2, 3, "h1", lambda: copy(yhi[:, 4:6, :], two(3), "tp", "ph"))
                boundary(2, 4, U_PLE)
                hi(U_PGATE + 2)
                pre_stats(4, 1, "h2")
                hi(U_PGATE + 3)
                for t in range(TOK):
                    after(f"ms{N_PRE[4]}_{t}")
                    after("pd") if t == 0 else used(U_PLE)
                    mean_square(ms(N_PLE, t), wide(PB[t]), D, gates[:, t, 0:D], f"ms{N_PLE}_{t}")
                for t in range(TOK):
                    after(f"rs{N_PRE[4]}_{t}")
                    after("gd") if t == 0 else used(UNITS - 1)
                    act.activation(gates[:, t, D:2 * D], wide(GB[t]), ACT.Sigmoid,
                                   scale=rs(N_PRE[4], t)).then_inc(sem(f"pg_{t}"), 1)

        @block.vector
        def _(dve):
            dve.memset(st[:, 0:40], 0.0).then_inc(sem("lo_ready"), RING)
            dve.memset(st[:, 40:80], 0.0).then_inc(sem("unit_used"), RING)
            dve.memset(st[:, 80:160], 0.0)
            dve.memset(lf[:, :, :, :], 0.0).then_inc(sem("lf0"), 1)
            dve.memset(qz[:, :, :], 0.0).then_inc(sem("qz0"), 1)
            dve.wait_ge(sem("x_in"), 16 * TOK)
            for t in range(TOK):
                dve.memset(zt[:, t], 0.0).then_inc(sem(f"h3_{t}"), 1)

            with dve.Fori(0, DEPTH) as L:
                L1 = dve.snap(L + 1)
                L16 = dve.snap(L * 16 + 16)
                U0 = dve.snap(L * UNITS)
                H0 = dve.snap(L * NCH)

                def after(name):
                    ev.wait(dve, name, L, L1)

                def used(u):
                    dve.wait_ge(sem("unit_used"), U0 + (u + 1 + RING))

                def lo(u, n=512, Uj=None):
                    dve.wait_ge(sem("hi_ready"), (U0 if Uj is None else Uj) + (u + 1))
                    d, a, b = (v[:, u % RING, :].rearrange("p (k n) -> p k n", k=4)[:, :, 0:n]
                               for v in (wlo, raw, whi))
                    dve.tensor_tensor(d, a, b, ALU.subtract).then_inc(sem("lo_ready"), 1)

                def minus(dst, a, b, wait, name):
                    after(wait)
                    dve.tensor_tensor(dst, a, b, ALU.subtract).then_inc(sem(name), 1)

                def transposed(e, t):
                    for half in range(2):
                        transposed_half(e, t, half)

                def transposed_half(e, t, half):
                    k, q = slice(4 * half, 4 * half + 4), slice(t * 128, (t + 1) * 128)
                    minus(xlo[:, k, q], two(TB[e][t][half], 4), xhi[:, k, q],
                          f"xhi{e}_{t}{half}", f"xlo{e}_{t}{half}")

                def premult(e, t, hname):
                    dve.wait_ge(sem(f"gpre{e}"), L16)
                    after(f"{hname}_{t}")
                    for half in range(2):
                        c = slice(512 * half, 512 * half + 512)
                        dve.tensor_tensor(hg[:, t, c], h[:, t, c], gpre[:, c], ALU.mult)\
                           .then_inc(sem(f"hg{e}_{t}{half}"), 1)

                def boundary(s, e, nxt):
                    for t in range(TOK):
                        after(f"gg{s}")
                        after(f"rs{s}_{t}")
                        dve.scalar_tensor_tensor(out=hg[:, t, :], in0=wide(FB[s] + 2 * t), scalar=rs(s, t),
                                                 in1=gpre[:, :], op0=ALU.mult, op1=ALU.mult)\
                           .then_inc(sem(f"n{s}_{t}"), 1)
                        after(f"n{s}_{t}")
                        for half in range(2):
                            c = slice(512 * half, 512 * half + 512)
                            dve.tensor_tensor(hg[:, t, c], hg[:, t, c], hpre[:, t, c], ALU.add)\
                               .then_inc(sem(f"hg{e}_{t}{half}"), 1)
                        transposed(e, t)
                        lo(nxt + 1 + t)

                def ffn(b, f, e, extra=None):
                    def act_up(tok, j):
                        dve.wait_ge(sem(f"silu{f}_{tok}"), j)
                        dve.scalar_tensor_tensor(out=hact[:, tok, :], in0=ps[:, tok, 256:512],
                                                 scalar=rs(N_PRE[e], tok), in1=silu[:, tok, :],
                                                 op0=ALU.mult, op1=ALU.mult).then_inc(sem(f"hact{f}_{tok}"), 1)

                    def hidden(j, buf):
                        dve.wait_ge(sem(f"hthi{f}"), j)
                        dve.tensor_tensor(ylo[:, 2 * buf:2 * buf + 2, :], two(2), yhi[:, 2 * buf:2 * buf + 2, :],
                                          ALU.subtract).then_inc(sem(f"htlo{f}"), 1)

                    act_up(0, H0 + 1)
                    lo(b + 3)
                    act_up(1, H0 + 1)
                    lo(b + 4)
                    hidden(H0 + 1, 0)
                    lo(b + 5)
                    for t in range(TOK):
                        act_up(t, H0 + 2)
                    lo(b + 6)
                    lo(b + 7)
                    with dve.Fori(2, NCH - 1) as j:
                        Hj = dve.snap(H0 + j)
                        Uj = dve.snap(U0 + j * 3)
                        hidden(Hj, 0)
                        lo(b + 2, Uj=Uj)
                        for t in range(TOK):
                            act_up(t, Hj + 1)
                        lo(b + 3, Uj=Uj)
                        lo(b + 4, Uj=Uj)
                    hidden(H0 + NCH - 1, 0)
                    if extra:
                        extra()
                    lo(b + 32)
                    for t in range(TOK):
                        act_up(t, H0 + NCH)
                    hidden(H0 + NCH, 1)
                    lo(b + 33)

                def softmax_in(p):
                    c = PIECE[p]
                    n, nk, v = len(c["heads"]), c["nk"], s_view(p)
                    after(f"sc_{p}")
                    if p[0] == "A":
                        m = maskA[:, SEQ - 128 * nk:].unsqueeze(1).to_broadcast([128, n, 128 * nk])
                    else:
                        m = bandD[:, c["heads"][0]:c["heads"][0] + n, SEQ - 128 * nk:]
                    dve.tensor_tensor(v, ps_view(p), m, ALU.add).then_inc(sem(f"sm_{p}"), 1)
                    after(f"sm_{p}")
                    dve.tensor_reduce(sums(p)[:, 0:n], v, AX.X, ALU.max).then_inc(sem(f"ma_{p}"), 1)
                    after(f"ma_{p}")
                    if p[0] == "A":
                        dve.tensor_scalar(mx(p)[:, 0:n], sums(p)[:, 0:n], -1.0, None, ALU.mult)\
                           .then_inc(sem(f"nm_{p}"), 1)
                        return
                    sk = snk[:, c["heads"][0]:c["heads"][0] + n]
                    dve.tensor_tensor(sums(p)[:, 0:n], sums(p)[:, 0:n], sk, ALU.max).then_inc(sem(f"mb_{p}"), 1)
                    after(f"mb_{p}")
                    dve.tensor_tensor(sexp[:, c["buf"], 0:n], sk, sums(p)[:, 0:n], ALU.subtract)
                    dve.tensor_scalar(mx(p)[:, 0:n], sums(p)[:, 0:n], -1.0, None, ALU.mult)\
                       .then_inc(sem(f"nm_{p}"), 1)

                def softmax_out(p):
                    c = PIECE[p]
                    n = len(c["heads"])
                    if p[0] == "D":
                        after(f"sx_{p}")
                        dve.tensor_tensor(sums(p)[:, 0:n], sums(p)[:, 0:n], sexp[:, c["buf"], 0:n], ALU.add)\
                           .then_inc(sem(f"sa_{p}"), 1)
                        after(f"sa_{p}")
                    else:
                        after(f"ex_{p}")
                    dve.reciprocal(sums(p)[:, 0:n], sums(p)[:, 0:n]).then_inc(sem(f"rc_{p}"), 1)

                def y_lo(p):
                    y0, n, q = yslice(p)
                    minus(ylo[:, y0:y0 + n, q:q + 128],
                          ps[:, PIECE[p]["pv"], 0:n * 128].rearrange("p (k n) -> p k n", k=n),
                          yhi[:, y0:y0 + n, q:q + 128], f"yh_{p}", f"yl_{p}")

                def tap(k, src, row, base, name, bias):
                    for c in range(2):
                        x, w = src[:, c, k:k + SEQ], cwT[:, c, row + k:row + k + 1]
                        if k == 0:
                            if bias:
                                ins = dve.tensor_scalar(acc[:, c, :], x, w, cwT[:, c, 34:35], ALU.mult, ALU.add)
                            else:
                                ins = dve.tensor_scalar(acc[:, c, :], x, w, None, ALU.mult)
                        else:
                            dve.wait_ge(sem(f"{name}{c}"), base + k)
                            ins = dve.scalar_tensor_tensor(out=acc[:, c, :], in0=x, scalar=w, in1=acc[:, c, :],
                                                           op0=ALU.mult, op1=ALU.add)
                        ins.then_inc(sem(f"{name}{c}"), 1)

                def branch(i, u, gate_slot, bank):
                    after(f"sig{i}")
                    for q in range(4):
                        quarter(i, u, gate_slot, bank, q)

                def quarter(i, u, gate_slot, bank, q):
                    after(f"br{i}_{q}") if q < 3 else used(u)
                    t, n = q // 2, q % 2
                    g = gates[:, t, gate_slot * D + n * 512:gate_slot * D + n * 512 + 512]
                    m = hg[:, t, n * 512:n * 512 + 512]
                    dve.tensor_tensor(m if i == 0 else g, ps[:, bank + q, :], g, ALU.mult)\
                       .then_inc(sem(f"gb{i}_{q}"), 1)
                    return m, g

                def last_branch(q):
                    m, g = quarter(3, U_BR_C, 1, 4, q)
                    after(f"add2_{q}")
                    after(f"gb3_{q}")
                    dve.tensor_tensor(m, m, g, ALU.add).then_inc(sem(f"merged_{q}"), 1)

                premult(0, 0, "h3")
                lo(0)
                transposed(0, 0)
                lo(1)
                premult(0, 1, "h3")
                transposed(0, 1)
                lo(2)
                ffn(U_FFN1, 1, 0)
                boundary(0, 1, U_HEAD)

                C0 = dve.snap(L * KC)
                B0 = dve.snap(L * KS)
                dve.wait_ge(sem("small"), dve.snap(L * (16 * 7)) + 16 * 7)
                for u in range(U_HEAD, U_WO + 4):
                    if u == 53:
                        y_lo("D0")
                    if u == 57:
                        softmax_out("D1a")
                    if u == 62:
                        after("t5")
                        dve.tensor_reduce(st[:, 146:148], two(6), AX.X, ALU.add).then_inc(sem("lnsum"), 1)
                        after("lnsum")
                        dve.tensor_scalar(st[:, 148:150], st[:, 146:148], -1.0 / CW, None, ALU.mult)\
                           .then_inc(sem("lnmean"), 1)
                        after("lnmean")
                        for t in range(TOK):
                            dve.tensor_scalar(lnx(t), two(6)[:, t, :], st[:, 148 + t:149 + t], None, ALU.add)\
                               .then_inc(sem(f"xc{t}"), 1)
                    if U_HEAD < u < U_WO + 3 and u != U_BR_C:
                        lo(u + 2, HEAD_COLS - 5 * 512 if u + 2 in (U_GATE1 - 2, U_GATE1 - 1) else 512)
                    if u == 50:
                        dve.wait_ge(sem("band"), L16)
                        softmax_in("D0")
                    if u == 56:
                        softmax_in("D1a")
                    if u == 62:
                        y_lo("D1b")
                    g = gate_chunk(u)
                    if g is not None:
                        dve.wait_ge(sem(f"gbias{g % 2}"), dve.snap(L * 128) + 32 * (g // 2 + 1))
                        if g == 6:
                            after("add1_3")
                        for t in range(TOK):
                            after(f"gate{g}") if t == 0 else used(u)
                            dve.scalar_tensor_tensor(
                                out=gates[:, t, (g % 4) * 512:(g % 4) * 512 + 512], in0=ps[:, 2 * (g % 2) + t, :],
                                scalar=rs(N_PRE[1], t), in1=gbias[:, g % 2, :],
                                op0=ALU.mult, op1=ALU.add).then_inc(sem("gate_pre"), 1)
                    if u == 37:
                        for t in range(TOK):
                            after(f"proj1_{t}")
                        dve.tensor_tensor(zt[:, 0], proj[:, :, C_F:C_F + AH],
                                          bfs[:, :].unsqueeze(1).to_broadcast([128, TOK, AH]), ALU.add)\
                           .then_inc(sem("z"), 1)
                    if u == 38:
                        after("zln")
                        dve.wait_ge(sem("masks"), 1)
                        dve.tensor_scalar(zt[:, 0], zt[:, 0], 0.0, None, ALU.min).then_inc(sem("zmin"), 1)
                        after("zmin")
                        dve.tensor_tensor(lf[:, :, 0, 0:AH], zt[:, 1], zt[:, 0], ALU.subtract)
                        dve.tensor_tensor(lf[:, :, 1, AH:2 * AH], zt[:, 0], zt[:, 1], ALU.subtract)\
                           .then_inc(sem("lf"), 1)
                    if u == 40:
                        after("cs")
                        dve.tensor_scalar(decR[:, :], ps[:, 6, 0:SEQ], cstc[:, 0:1], None, ALU.add)
                        for hh in range(AH):
                            ins = dve.tensor_scalar(decL[:, hh, :], ps[:, 6, SEQ:], cstc[:, 1:2],
                                                    cstc[:, 2 + hh:3 + hh], ALU.add, ALU.mult)
                        ins.then_inc(sem("dec"), 1)
                        after("tcw")
                        dve.tensor_copy(cwT[:, :, :], ps[:, 7, 0:70].rearrange("p (k n) -> p k n", k=2))\
                           .then_inc(sem("cw"), 1)
                    if u == 42:
                        softmax_in("A0")
                        softmax_in("A1")
                        softmax_out("A0")
                        softmax_out("A1")
                    if u == 45:
                        y_lo("A0")
                    if u == 46:
                        y_lo("A1")
                    if u == 48:
                        after("uT")
                        after("cw")
                        dve.memset(upad[:, :, 0:KS - 1], 0.0).then_inc(sem("pad0"), 1)
                        after("pad0")
                        for k in range(KS):
                            tap(k, upad, KC, B0, "cb", False)
                        after("bgT")
                        for c in range(2):
                            dve.wait_ge(sem(f"cb{c}"), B0 + KS)
                        dve.tensor_tensor(acc[:, :, :], acc[:, :, :], bgT[:, :, :], ALU.mult).then_inc(sem("yb"), 1)
                    if u == 50:
                        minus(ylo[:, Y[1]:Y[1] + 2, :], acc[:, :, :], yhi[:, Y[1]:Y[1] + 2, :], "ybh", "ybl")
                        softmax_out("D0")
                    if u == 51:
                        after("gT")
                        dve.memset(gpad[:, :, 0:KC - 1], 0.0).then_inc(sem("pad1"), 1)
                        after("ybl")
                        after("pad1")
                    if u == 57:
                        softmax_in("D1b")
                    if u == 58:
                        softmax_out("D1b")
                    if u == 60:
                        y_lo("D1a")
                    if u == 53:
                        branch(0, U_BR_B, 0, 0)
                    if u == 54:
                        branch(1, U_BR_A, 1, 4)
                    if 51 <= u < 51 + len(TAPS):
                        k0 = sum(TAPS[:u - 51])
                        for k in range(k0, k0 + TAPS[u - 51]):
                            tap(k, gpad, 0, C0, "cc", True)
                    if u == 62:
                        for t in range(TOK):
                            after(f"rs{N_LN}_{t}")
                            dve.scalar_tensor_tensor(out=lnx(t), in0=lnx(t), scalar=rs(N_LN, t), in1=lnp[:, 0, :],
                                                     op0=ALU.mult, op1=ALU.mult).then_inc(sem(f"lng{t}"), 1)
                    if u == 64:
                        minus(ylo[:, Y[2]:Y[2] + 2, :], two(7), yhi[:, Y[2]:Y[2] + 2, :], "ych", "ycl")
                        branch(2, U_BR_D + 1, 0, 0)
                    if u == U_BR_C:
                        after("sig3")
                        last_branch(0)
                        last_branch(1)
                        transposed_half(2, 0, 0)
                        last_branch(2)
                        lo(u + 2)
                        transposed_half(2, 0, 1)
                        last_branch(3)
                        transposed(2, 1)
                boundary(1, 3, U_FFN2)

                ffn(U_FFN2, 2, 3, lambda: minus(ylo[:, 4:6, :], two(3), yhi[:, 4:6, :], "ph", "pl"))
                boundary(2, 4, U_PLE)
                for u in range(U_PGATE + 2, UNITS):
                    lo(u)
                dve.wait_ge(sem("gpost3"), L16)
                for t in range(TOK):
                    after(f"rs{N_PLE}_{t}")
                    dve.scalar_tensor_tensor(out=gates[:, t, 0:D], in0=wide(PB[t]), scalar=rs(N_PLE, t),
                                             in1=gpost[:, :], op0=ALU.mult, op1=ALU.mult).then_inc(sem(f"pn_{t}"), 1)
                after("pn_0")
                after("pg_0")
                dve.tensor_tensor(gates[:, 0, 0:D], gates[:, 0, 0:D], gates[:, 0, D:2 * D], ALU.mult)\
                   .then_inc(sem("pp_0"), 1)
                after("pp_0")
                dve.tensor_tensor(h[:, 0, :], h[:, 0, :], gates[:, 0, 0:D], ALU.add).then_inc(sem("h3_0"), 1)

        @block.gpsimd
        def _(pool):
            pool.memset(epsc[:, 0:4], EPS).then_inc(sem("c_eps"), 1)
            pool.memset(epsc[:, 4:8], -0.5).then_inc(sem("c_half"), 1)
            pool.memset(epsc[:, 8:12], 0.5).then_inc(sem("c_half"), 1)
            pool.memset(ident[:, :], 0.0).then_inc(sem("c_id"), 1)
            pool.memset(cumU[:, :], 1.0).then_inc(sem("c_u"), 1)
            pool.memset(maskA[:, :], 0.0).then_inc(sem("c_m"), 1)
            pool.memset(cstc[:, 0:2], 1.0).then_inc(sem("c_c"), 1)
            pool.memset(cstc[:, 2:8], 0.0).then_inc(sem("c_c"), 1)
            for name, n in (("c_eps", 1), ("c_half", 2), ("c_id", 1), ("c_u", 1), ("c_m", 1), ("c_c", 2)):
                pool.wait_ge(sem(name), n)

            def select(ap, op, fill, base, pattern, cm):
                return pool.affine_select(out=ap, in_=ap, compare_op=op, fill=fill, base=base, pattern=pattern,
                                          channel_multiplier=cm)

            select(ident[:, :], ALU.not_equal, 1.0, 0, [[-1, 128]], 1).then_inc(sem("ident"), 1)
            select(cumU[:, :], ALU.is_ge, 0.0, 0, [[1, SEQ]], -1)
            select(maskA[:, :], ALU.is_ge, NEG, 128, [[-1, SEQ]], 1)
            select(cstc[:, 0:1], ALU.is_ge, 0.0, -AH, [[0, 1]], 1).then_inc(sem("c_c"), 1)
            select(cstc[:, 1:2], ALU.is_ge, 0.0, AH - 1, [[0, 1]], -1).then_inc(sem("c_c"), 1)
            select(cstc[:, 2:6], ALU.not_equal, 1.0, 0, [[-1, AH]], 1).then_inc(sem("c_c"), 1)
            pool.wait_ge(sem("c_c"), 5)
            select(cstc[:, 0:1], ALU.is_ge, 0.0, 2 * AH - 1, [[0, 1]], -1).then_inc(sem("c_c"), 1)
            pool.wait_ge(sem("c_c"), 6)
            select(cstc[:, 2:6], ALU.not_equal, 1.0, -AH, [[-1, AH]], 1).then_inc(sem("masks"), 1)

            pool.memset(relrow, NEG).then_inc(sem("rel0"), 1)
            pool.wait_ge(sem("rel0"), 1)
            pool.wait_ge(sem("rel_in"), 16)
            lo_d = 0
            while lo_d < WINDOW:
                hi_d = lo_d
                while hi_d < WINDOW and bucket(hi_d) == bucket(lo_d):
                    hi_d += 1
                b = bucket(lo_d)
                ins = pool.tensor_copy(relrow[:, 256 - hi_d:256 - lo_d],
                                      relT[:, b:b + 1].to_broadcast([DH, hi_d - lo_d]))
                lo_d = hi_d
            ins.then_inc(sem("relrow"), 1)
            pool.wait_ge(sem("relrow"), 1)
            pool.dma_start(relscr[:, :, :], relrow.unsqueeze(1).to_broadcast([DH, 128, 512])).then_inc(sem("relscr"), 16)

            with pool.Fori(0, DEPTH) as L:
                L1 = pool.snap(L + 1)
                L16 = pool.snap(L * 16 + 16)

                def after(name):
                    ev.wait(pool, name, L, L1)

                def root(s, ts=range(TOK)):
                    for t in ts:
                        after(f"ms{s}_{t}")
                        pool.tensor_tensor(ve(s, t), ms(s, t), epsc[:, 0:1], ALU.add).then_inc(sem(f"ve{s}_{t}"), 1)
                        after(f"ve{s}_{t}")
                        pool.tensor_tensor(rs(s, t), ve(s, t), epsc[:, 4:5], ALU.pow).then_inc(sem(f"rs{s}_{t}"), 1)

                def tt(dst, a, b, op, name):
                    pool.tensor_tensor(dst, a, b, op).then_inc(sem(name), 1)

                def gains(s, e):
                    if s == 1:
                        after("merged_3")
                    pool.wait_ge(sem(f"gpre{e}"), L16)
                    for t in range(TOK):
                        tt(hpre[:, t, :], h[:, t, :], gpre[:, :], ALU.mult, f"hp{s}_{t}")
                    pool.wait_ge(sem(f"gpost{s}"), L16)
                    if s != 1:
                        tt(gpost[:, :], gpost[:, :], epsc[:, 8:9].to_broadcast([128, D]), ALU.mult, f"gh{s}")
                        after(f"gh{s}")
                    after(f"hp{s}_1")
                    tt(gpre[:, :], gpre[:, :], gpost[:, :], ALU.mult, f"gg{s}")

                def residual(s, e):
                    def scale(t):
                        after(f"tm{s}_{t}")
                        tt(tmp[:, t, :], tmp[:, t, :], gpost[:, :], ALU.mult, f"tg{s}_{t}")

                    def add(t):
                        after(f"tg{s}_{t}")
                        tt(h[:, t, :], h[:, t, :], tmp[:, t, :], ALU.add, f"h{s}_{t}")

                    root(s)
                    scale(0)
                    add(0)
                    scale(1)
                    root(N_PRE[e], [0])
                    add(1)
                    root(N_PRE[e], [1])

                def normalise(p):
                    after(f"rc_{p}")
                    v = s_view(p)
                    n, w = len(PIECE[p]["heads"]), 128 * PIECE[p]["nk"]
                    tt(v, v, sums(p)[:, 0:n].unsqueeze(2).to_broadcast([128, n, w]), ALU.mult, f"pn_{p}")

                def add_branch(i, gate_slot):
                    for q in range(4):
                        after(f"gb{i}_{q}")
                        t, n = q // 2, q % 2
                        m = hg[:, t, n * 512:n * 512 + 512]
                        tt(m, m, gates[:, t, gate_slot * D + n * 512:gate_slot * D + n * 512 + 512], ALU.add,
                           f"add{i}_{q}")

                root(N_PRE[0])
                gains(0, 1)
                residual(0, 1)
                normalise("A0")
                normalise("A1")
                for t in range(TOK):
                    after(f"proj3_{t}")
                xb = proj[:, :, C_XB:C_XB + CW]
                tt(xb, xb, proj[:, :, C_CG:C_CG + CW], ALU.mult, "cgxb")
                after("csig")
                tt(lnx2, lnx2, lnj2, ALU.mult, "glu")
                normalise("D0")
                add_branch(1, 1)
                normalise("D1a")
                normalise("D1b")
                root(N_LN)
                for t in range(TOK):
                    after(f"lng{t}")
                tt(lnx2, lnx2, lnp[:, 1, :].unsqueeze(1).to_broadcast([128, TOK, CW]), ALU.add, "lny")
                after("lnsig")
                tt(lnx2, lnx2, lnj2, ALU.mult, "lnm")
                add_branch(2, 0)
                gains(1, 3)
                residual(1, 3)
                gains(2, 4)
                residual(2, 4)
                root(N_PLE)
                after("pn_1")
                after("pg_1")
                tt(gates[:, 1, 0:D], gates[:, 1, 0:D], gates[:, 1, D:2 * D], ALU.mult, "pp_1")
                after("pp_1")
                tt(h[:, 1, :], h[:, 1, :], gates[:, 1, 0:D], ALU.add, "h3_1")

        @block.tensor
        def _(pe):
            with pe.Fori(0, DEPTH) as L:
                L1 = pe.snap(L + 1)
                U0 = pe.snap(L * UNITS)
                H0 = pe.snap(L * NCH)
                G0 = pe.snap(L * 16)

                def after(name):
                    ev.wait(pe, name, L, L1)

                def split(u, Uj=None):
                    pe.wait_ge(sem("lo_ready"), (U0 if Uj is None else Uj) + (u + 1 + RING))

                def mm(out_, lhsT, rhs, start, stop):
                    return nc.tensor.matmul(out_, lhsT, rhs, start=start, stop=stop, skip_group_check=True)

                def mm3(outs, lh, ll, rh, rl, start, stop):
                    for i, o in enumerate(outs):
                        mm(o, lh, rh[i], start, False)
                    for i, o in enumerate(outs):
                        mm(o, lh, rl[i], False, False)
                    for i, o in enumerate(outs):
                        ins = mm(o, ll, rh[i], False, stop)
                    return ins

                def unit_cols(u, half, t, bank, n=512, ks=range(4)):
                    q = slice(t * 128, (t + 1) * 128)
                    for k in ks:
                        kt = 4 * half + k
                        w = slice(512 * k, 512 * k + n)
                        ins = mm3([ps[:, bank, 0:n]], xhi[:, kt, q], xlo[:, kt, q],
                                  [whi[:, u % RING, w]], [wlo[:, u % RING, w]], kt == 0, kt == KT - 1)
                    return ins

                def unit_rows(u, xh, xl, kt0, t, bank, first, last, quarter=None, ks=range(2)):
                    q = slice(t * 128, (t + 1) * 128)
                    sl = u % RING
                    for k in ks:
                        w = [slice(D * k + 512 * n, D * k + 512 * n + 512) for n in range(2)]
                        if quarter is not None and last and k == 1:
                            for n in range(2):
                                ins = mm3([ps[:, bank + n, :]], xh[:, kt0 + k, q], xl[:, kt0 + k, q],
                                          [whi[:, sl, w[n]]], [wlo[:, sl, w[n]]], False, True)
                                if 2 * t + n < 3:
                                    ins.then_inc(sem(f"br{quarter}_{2 * t + n}"), 1)
                            return ins
                        ins = mm3([ps[:, bank + n, :] for n in range(2)], xh[:, kt0 + k, q], xl[:, kt0 + k, q],
                                  [whi[:, sl, x] for x in w], [wlo[:, sl, x] for x in w],
                                  first and k == 0, last and k == 1)
                    return ins

                def done(ins):
                    ins.then_inc(sem("unit_used"), 1)

                def transpose(dst, src):
                    n = src.shape[0]
                    return nc.tensor.transpose(dst, src, ident[0:n, 0:n])

                def turn_half(e, t, half, src, ready, bank_free):
                    after(ready)
                    if bank_free:
                        after(bank_free)
                    for k in range(4):
                        c = 512 * half + 128 * k
                        ins = transpose(two(TB[e][t][half], 4)[:, k, :], src[:, t, c:c + 128])
                    ins.then_inc(sem(f"xt{e}_{t}{half}"), 1)

                def turn_hg(e, t):
                    for half in range(2):
                        turn_half(e, t, half, hg, f"hg{e}_{t}{half}", f"xlo{e}_0{half}" if t else None)

                def first_chunk(b, e, name):
                    for t in range(TOK):
                        for half in range(2):
                            after(f"xlo{e}_{t}{half}")
                            split(b + half)
                            if (t, half) == (0, 1):
                                unit_cols(b + half, half, t, t, ks=range(3))
                                turn_hg(e, 1)
                                unit_cols(b + half, half, t, t, ks=[3]).then_inc(sem(name), 1)
                            else:
                                ins = unit_cols(b + half, half, t, t)
                            if t == 1:
                                done(ins)

                def ffn(b, f, e, extra=None):
                    def chunk(j, u, Uj=None):
                        split(u, Uj)
                        for t in range(TOK):
                            pe.wait_ge(sem(f"hact{f}_{t}"), j)
                            ins = unit_cols(u, 0, t, t)
                        done(ins)

                    def chunk_b(u, Uj=None):
                        split(u, Uj)
                        for t in range(TOK):
                            ins = unit_cols(u, 1, t, t)
                            if t == 0:
                                ins.then_inc(sem(f"gu{f}"), 1)
                        done(ins)

                    def hidden(j):
                        for t in range(TOK):
                            pe.wait_ge(sem(f"hact{f}_{t}"), j)
                        for k in range(2):
                            for t in range(TOK):
                                ins = transpose(two(2)[:, k, t * 128:(t + 1) * 128], hact[:, t, 128 * k:128 * k + 128])
                        ins.then_inc(sem(f"ht{f}"), 1)

                    def down(u, t, buf, first, last, ks=range(2)):
                        return unit_rows(u, yhi, ylo, 2 * buf, t, 4 + 2 * t, first, last, ks=ks)

                    first_chunk(b, e, f"gu{f}")
                    chunk(H0 + 1, b + 2)
                    hidden(H0 + 1)
                    chunk_b(b + 3)
                    pe.wait_ge(sem(f"htlo{f}"), H0 + 1)
                    split(b + 4)
                    for t in range(TOK):
                        ins = down(b + 4, t, 0, True, False)
                    done(ins)
                    with pe.Fori(2, NCH - 1) as j:
                        Hj = pe.snap(H0 + j)
                        Uj = pe.snap(U0 + j * 3)
                        chunk(Hj, b - 1, Uj)
                        hidden(Hj)
                        chunk_b(b, Uj)
                        pe.wait_ge(sem(f"htlo{f}"), Hj)
                        split(b + 1, Uj)
                        for t in range(TOK):
                            ins = down(b + 1, t, 0, False, False)
                        done(ins)
                    chunk(H0 + NCH - 1, b + 29)
                    hidden(H0 + NCH - 1)
                    if extra:
                        extra()
                    chunk_b(b + 30)
                    pe.wait_ge(sem(f"htlo{f}"), H0 + NCH - 1)
                    split(b + 31)
                    down(b + 31, 0, 0, False, False, [0])
                    hidden(H0 + NCH)
                    down(b + 31, 0, 0, False, False, [1])
                    pe.wait_ge(sem(f"htlo{f}"), H0 + NCH)
                    if extra:
                        after("pl")
                    split(b + 32)
                    down(b + 32, 0, 1, False, True).then_inc(sem(f"f{0 if f == 1 else 2}_0"), 1)
                    done(down(b + 31, 1, 0, False, False))
                    down(b + 32, 1, 1, False, True, [0])
                    turn_hg(1 if f == 1 else 4, 0)
                    done(down(b + 32, 1, 1, False, True, [1]))

                def scores(p):
                    c = PIECE[p]
                    v = ps_view(p)
                    q = slice(128 * c["qb"], 128 * c["qb"] + 128)
                    keys = slice(0, 128 * c["nk"])
                    for i, hh in enumerate(c["heads"]):
                        if p[0] == "A":
                            mm(v[:, i, :], qz[:, hh, q], kz[:, hh // 2, keys], True, False)
                            ins = mm(v[:, i, :], decL[:, hh, q], decR[:, keys], False, True)
                        else:
                            ins = mm(v[:, i, :], qz[:, hh, q], kz[:, hh // DG, keys], True, True)
                    ins.then_inc(sem(f"sc_{p}"), 1)

                def probs_t(p, r, wait):
                    c = PIECE[p]
                    after(f"pn_{p}")
                    if wait:
                        after(wait)
                    blocks = [(i, k) for i in range(len(c["heads"])) for k in range(c["nk"])][4 * r:4 * r + 4]
                    for n, (i, k) in enumerate(blocks):
                        ins = transpose(two(c["pt"][r], 4)[:, n, :], s_view(p)[:, i, 128 * k:128 * k + 128])
                    ins.then_inc(sem(f"tp_{p}_{r}"), 1)

                def values(p, rounds):
                    c = PIECE[p]
                    for r in range(rounds):
                        after(f"te_{p}_{r}")
                    for i, hh in enumerate(c["heads"]):
                        c0 = C_VA + hh * HD if p[0] == "A" else C_VD + (hh // DG) * HD
                        rows_ = slice(64 * (i % 2), 64 * (i % 2) + 64)
                        for k in range(c["nk"]):
                            ins = mm(ps[rows_, c["pv"], (i // 2) * 128:(i // 2) * 128 + 128],
                                     proj[:, k, c0:c0 + HD], PT[:, i * c["nk"] + k, :], k == 0, k == c["nk"] - 1)
                    ins.then_inc(sem(f"pv_{p}"), 1)

                def turn_cols(bank, cols, name):
                    for k, src in enumerate(cols):
                        for t in range(TOK):
                            ins = transpose(two(bank)[:, k, t * 128:(t + 1) * 128], src(t))
                    if name:
                        ins.then_inc(sem(name), 1)

                def pcol(c0):
                    return lambda t: proj[:, t, c0:c0 + 128]

                pe.wait_ge(sem("ident"), 1)
                turn_hg(0, 0)
                ffn(U_FFN1, 1, 0)

                first_chunk(U_HEAD, 1, "head0")
                for u in range(U_HEAD + 2, U_WO):
                    if u < U_GATE1:
                        c, half = (u - U_HEAD) // 2, (u - U_HEAD) % 2
                        n = min(512, HEAD_COLS - 512 * c)
                        split(u)
                        for t in range(TOK):
                            if half == 0 and c >= 2:
                                after(f"proj{c - 2}_{t}")
                            ins = unit_cols(u, half, t, 2 * (c % 2) + t, n)
                            if t == 0 and half == 1:
                                ins.then_inc(sem(f"head{c}"), 1)
                        done(ins)
                    elif u < U_BR_B or U_GATE2 <= u < U_BR_D:
                        g, half = ((u - U_GATE1) // 2, (u - U_GATE1) % 2) if u < U_BR_B else \
                                  ((u - U_GATE2) // 2 + 4, (u - U_GATE2) % 2)
                        split(u)
                        for t in range(TOK):
                            if half == 0:
                                if g < 2:
                                    after(f"proj{4 + g}_{t}")
                                elif g in (4, 5):
                                    after(f"gb0_{2 * (g - 4) + t}")
                                else:
                                    pe.wait_ge(sem("gate_pre"), G0 + (2 * (g - 2) + t + 1))
                            ins = unit_cols(u, half, t, 2 * (g % 2) + t)
                            if t == 0 and half == 1:
                                ins.then_inc(sem(f"gate{g}"), 1)
                        done(ins)
                    elif u == U_BR_B:
                        split(u)
                        after("ybl")
                        for t in range(TOK):
                            pe.wait_ge(sem("gate_pre"), G0 + (6 + 2 * t))
                            ins = unit_rows(u, yhi, ylo, Y[1], t, 2 * t, True, True, 0)
                        done(ins)
                    elif u == U_BR_A:
                        split(u)
                        for name in ("yl_A1", "yl_D0", "kD", "gT"):
                            after(name)
                        for t in range(TOK):
                            ins = unit_rows(u, yhi, ylo, Y[0], t, 4 + 2 * t, True, True, 1)
                        done(ins)
                    elif u < U_BR_C:
                        i = u - U_BR_D
                        split(u)
                        if i == 0:
                            after("yl_D1b")
                        for t in range(TOK):
                            if i == 0:
                                pe.wait_ge(sem("gate_pre"), G0 + (14 + 2 * t))
                            elif t == 1:
                                after("lnm")
                                turn_cols(7, [pcol(C_CA), pcol(C_CA + 128)], "t6")
                            ins = unit_rows(u, yhi, ylo, Y[3] + 2 * i, t, 2 * t, i == 0, i == 1, 2)
                        done(ins)
                    else:
                        split(u)
                        after("ycl")
                        unit_rows(u, yhi, ylo, Y[2], 0, 4, True, True, 3)
                        unit_rows(u, yhi, ylo, Y[2], 1, 6, True, False, ks=[0])
                        turn_half(2, 0, 0, hg, "merged_0", None)
                        ins = unit_rows(u, yhi, ylo, Y[2], 1, 6, False, True, 3, ks=[1])
                        done(ins)

                    if u == 38:
                        for t in range(TOK):
                            after(f"proj0_{t}")
                        turn_cols(4, [pcol(C_QA), pcol(C_QA + 128)], None)
                        turn_cols(5, [pcol(C_KA), pcol(C_KA + 128)], "tA")
                    if u == 39:
                        pe.wait_ge(sem("small"), pe.snap(L * (16 * 7)) + 16 * 7)
                        after("lf")
                        for i in range(2):
                            mm(ps[:, 6, SEQ * i:SEQ * i + SEQ], lf[:, 0, i, :], cumU[:, :], True, False)
                            ins = mm(ps[:, 6, SEQ * i + 128:SEQ * i + SEQ], lf[:, 1, i, :], cumU[:, 0:128],
                                     False, True)
                        ins.then_inc(sem("cs"), 1)
                        for c in range(2):
                            ins = transpose(ps[:, 7, 35 * c:35 * c + 35], cwrow[:, 128 * c:128 * c + 128])
                        ins.then_inc(sem("tcw"), 1)
                    if u == 41:
                        for name in ("qA", "kA", "dec"):
                            after(name)
                        scores("A0")
                        scores("A1")
                    if u == 43:
                        probs_t("A0", 0, "cw")
                    if u == 44:
                        values("A0", 1)
                        probs_t("A1", 0, None)
                        probs_t("A1", 1, None)
                    if u == 45:
                        values("A1", 2)
                    if u == 46:
                        after("cgxb")
                        after("yl_A0")
                        turn_cols(4, [pcol(C_XB), pcol(C_XB + 128)], None)
                        turn_cols(5, [pcol(C_BG), pcol(C_BG + 128)], "tB")
                    if u == 47:
                        after("yl_A1")
                        turn_cols(6, [pcol(C_QD), pcol(C_QD + 128)], None)
                        turn_cols(7, [pcol(C_QD + 256), pcol(C_QD + 384)], "tD")
                    if u == 48:
                        after("uT")
                        after("kdup")
                        turn_cols(4, [lambda t, g=g: kdup[:, t, g].rearrange("p r d -> p (r d)") for g in range(2)],
                                  "tDk")
                        after("bgT")
                        after("glu")
                        turn_cols(5, [pcol(C_CA), pcol(C_CA + 128)], "tC")
                    if u == 49:
                        after("qD1")
                        after("kD")
                        scores("D0")
                    if u == 51:
                        after("gT")
                        probs_t("D0", 0, None)
                        probs_t("D0", 1, None)
                    if u == 52:
                        values("D0", 2)
                    if u == 55:
                        after("gb1_0")
                        after("gb1_1")
                        scores("D1a")
                    if u == 56:
                        after("gb1_2")
                        after("gb1_3")
                        scores("D1b")
                    if u == 58:
                        probs_t("D1a", 0, None)
                        probs_t("D1a", 1, None)
                    if u == 59:
                        values("D1a", 2)
                    if u == 60:
                        probs_t("D1b", 0, None)
                        probs_t("D1b", 1, None)
                    if u == 61:
                        values("D1b", 2)
                        for c in range(2):
                            pe.wait_ge(sem(f"cc{c}"), pe.snap(L * KC) + KC)
                        for t in range(TOK):
                            for c in range(2):
                                ins = transpose(two(6)[:, t, 128 * c:128 * c + 128],
                                                acc[:, c, t * 128:(t + 1) * 128])
                        ins.then_inc(sem("t5"), 1)

                for n, (i, t) in enumerate(((0, 0), (1, 0), (0, 1), (1, 1), (2, 0), (3, 0), (2, 1), (3, 1))):
                    u = U_WO + i
                    split(u)
                    if n == 0:
                        turn_half(2, 0, 1, hg, "merged_1", None)
                    after(f"xlo2_{t}{i // 2}")
                    ins = unit_rows(u, xhi, xlo, 2 * i, t, FB[1] + 2 * t, i == 0, i == 3,
                                    ks=[0] if n == 7 else range(2))
                    if n < 2:
                        turn_half(2, 1, n, hg, f"merged_{2 + n}", None)
                    if n == 7:
                        turn_hg(3, 0)
                        ins = unit_rows(u, xhi, xlo, 2 * i, t, FB[1] + 2 * t, False, True, ks=[1])
                    if t == 1:
                        done(ins)
                    elif i == 3:
                        ins.then_inc(sem("f1_0"), 1)

                def p_turn():
                    pe.wait_ge(sem("p_in"), pe.snap(L * 16) + 16)
                    turn_cols(3, [lambda t: pin[:, t, 0:128], lambda t: pin[:, t, 128:256]], "tp")

                ffn(U_FFN2, 2, 3, p_turn)
                split(U_PLE)
                after("pl")
                for t in range(TOK):
                    if t == 1:
                        after("tm2_0")
                    ins = unit_rows(U_PLE, yhi, ylo, 4, t, PB[t], True, True)
                    if t == 0:
                        ins.then_inc(sem("pd"), 1)
                    else:
                        done(ins)
                for i, t in ((0, 0), (0, 1), (1, 0), (1, 1), (2, 0), (3, 0), (2, 1), (3, 1)):
                    split(U_PGATE + i)
                    if i == 0:
                        after("xlo4_11" if t else "tm2_1")
                    if (i, t) == (0, 0):
                        unit_rows(U_PGATE, xhi, xlo, 0, 0, GB[0], True, False, ks=[0])
                        turn_hg(4, 1)
                        unit_rows(U_PGATE, xhi, xlo, 0, 0, GB[0], False, False, ks=[1])
                        continue
                    ins = unit_rows(U_PGATE + i, xhi, xlo, 2 * i, t, GB[t], i == 0, i == 3)
                    if t == 1:
                        done(ins)
                    elif i == 3:
                        ins.then_inc(sem("gd"), 1)


INPUTS = ["x", "p", "ffn1_norm_pre", "ffn1_w_gu", "ffn1_w_down", "ffn1_norm_post", "mix_norm_pre", "w_in",
          "b_forget", "b_gate", "conv_short", "conv_dw", "conv_dw_bias", "conv_ln_gain", "conv_ln_bias",
          "attn_sinks", "rel_bias", "w_br_a", "w_br_b", "w_br_c", "w_br_d", "w_o", "mix_norm_post",
          "ffn2_norm_pre", "ffn2_w_gu", "ffn2_w_down", "ffn2_norm_post", "ple_norm_gate", "w_ple_gate",
          "w_ple", "ple_norm_post"]


def kernel(**inputs):
    import concourse.bacc as bacc
    from concourse.bass_utils import run_bass_kernel_spmd

    nc = bacc.Bacc("TRN2", target_bir_lowering=False, num_devices=1)
    arrays, aps = {}, {}
    for name in INPUTS:
        a = np.ascontiguousarray(inputs[name])
        arrays[f"in_{name}"] = a
        aps[name] = nc.dram_tensor(f"in_{name}", a.shape, mybir.dt.from_np(a.dtype), kind="ExternalInput").ap()
    out = nc.dram_tensor("out_0", (1, SEQ, D), F32, kind="ExternalOutput").ap()
    build(nc, aps, out)
    r = run_bass_kernel_spmd(nc, [arrays], core_ids=[0])
    return r.results[0]["out_0"]
```
